# Optimizing a Trainium2 kernel written in Bass

```python
import jax, jax.numpy as jnp
from jax import lax
import numpy as np

D_MODEL = 1024
BATCH = 1
SEQ = 1024
DEPTH = 2
DEC_BATCH = 8
DEC_SEQ = 1
PAST_LEN = 1024
PAGE_SIZE = 128

N_MIXERS = 2
N_ATTN_LAYERS = (DEPTH + N_MIXERS - 1) // N_MIXERS
N_RET_LAYERS = DEPTH // N_MIXERS
ATTN_HEAD_DIM = 64
ATTN_HEADS = D_MODEL // ATTN_HEAD_DIM
ATTN_KV_HEADS = 4
WINDOW = 128
ROPE_THETA = 10000.0
RET_KEY_DIM = 256
RET_HEADS = D_MODEL // RET_KEY_DIM
RET_VALUE_DIM = 2 * RET_KEY_DIM
RET_CHUNK = 128
D_FF = 256 * ((8 * D_MODEL // 3 + 255) // 256)
CONV_WIDTH = 3
LN_EPS = 1e-5
GN_EPS = 1e-5
DEEPNORM_ALPHA = (2.0 * DEPTH) ** 0.25
DEEPNORM_BETA = (8.0 * DEPTH) ** -0.25

kernel_name = 'swa_sink_retention_convffn_step'

def layer_norm(x, g, b):
    xf = x.astype(jnp.float32)
    mu = jnp.mean(xf, axis=-1, keepdims=True)
    var = jnp.mean(jnp.square(xf - mu), axis=-1, keepdims=True)
    return ((xf - mu) * lax.rsqrt(var + LN_EPS) * g + b).astype(x.dtype)

def rope(x, pos):
    half = x.shape[-1] // 2
    inv_freq = ROPE_THETA ** (-jnp.arange(half, dtype=jnp.float32) / half)
    ang = pos.astype(jnp.float32)[:, None] * inv_freq[None, :]
    cos = jnp.cos(ang)[:, None, :]
    sin = jnp.sin(ang)[:, None, :]
    xf = x.astype(jnp.float32)
    x1, x2 = xf[..., :half], xf[..., half:]
    return jnp.concatenate([x1 * cos - x2 * sin, x2 * cos + x1 * sin], axis=-1).astype(x.dtype)

def retention_rotate(x, pos):
    d = x.shape[-1]
    angle = 1.0 / (10000.0 ** jnp.linspace(0.0, 1.0, d // 2, dtype=jnp.float32))
    ang = pos.astype(jnp.float32)[:, None] * angle[None, :]
    cos = jnp.cos(ang)[:, None, :]
    sin = jnp.sin(ang)[:, None, :]
    x1, x2 = x[..., 0::2], x[..., 1::2]
    return jnp.stack([x1 * cos - x2 * sin, x2 * cos + x1 * sin], axis=-1).reshape(x.shape)

def sink_attention(q, k, v, qpos, kpos, sinks):
    lead = q.shape[:-3]
    tq = q.shape[-3]
    group = ATTN_HEADS // ATTN_KV_HEADS
    qg = q.reshape(*lead, tq, ATTN_KV_HEADS, group, ATTN_HEAD_DIM)
    s = jnp.einsum('...qkgd,...skd->...kgqs', qg, k).astype(jnp.float32) * (ATTN_HEAD_DIM ** -0.5)
    rel = qpos[..., :, None] - kpos[..., None, :]
    valid = (kpos[..., None, :] >= 0) & (rel >= 0) & (rel <= WINDOW)
    s = jnp.where(valid[..., None, None, :, :], s, -jnp.inf)
    sink = sinks.astype(jnp.float32).reshape(ATTN_KV_HEADS, group, 1, 1)
    m = jnp.maximum(jnp.max(s, axis=-1, keepdims=True), sink)
    p = jnp.exp(s - m)
    w = p / (jnp.sum(p, axis=-1, keepdims=True) + jnp.exp(sink - m))
    o = jnp.einsum('...kgqs,...skd->...qkgd', w.astype(v.dtype), v)
    return o.reshape(*lead, tq, ATTN_HEADS, ATTN_HEAD_DIM)

def attn_project(x, w_qkv):
    b, t, _ = x.shape
    qkv = x @ w_qkv
    nq = ATTN_HEADS * ATTN_HEAD_DIM
    nkv = ATTN_KV_HEADS * ATTN_HEAD_DIM
    q = qkv[..., :nq].reshape(b, t, ATTN_HEADS, ATTN_HEAD_DIM)
    k = qkv[..., nq:nq + nkv].reshape(b, t, ATTN_KV_HEADS, ATTN_HEAD_DIM)
    v = qkv[..., nq + nkv:].reshape(b, t, ATTN_KV_HEADS, ATTN_HEAD_DIM)
    return q, k, v

def swa_prompt(x, w_qkv, sinks, w_o):
    b, t, _ = x.shape
    nb = t // WINDOW
    pos = jnp.arange(t)
    q, k, v = attn_project(x, w_qkv)
    q = rope(q, pos)
    k = rope(k, pos)

    def band(z):
        zb = z.reshape(b, nb, WINDOW, ATTN_KV_HEADS, ATTN_HEAD_DIM)
        prev = jnp.concatenate([jnp.zeros_like(zb[:, :1]), zb[:, :-1]], axis=1)
        return jnp.concatenate([prev, zb], axis=2)

    qb = q.reshape(b, nb, WINDOW, ATTN_HEADS, ATTN_HEAD_DIM)
    qpos = pos.reshape(nb, WINDOW)
    kpos = qpos[:, :1] - WINDOW + jnp.arange(2 * WINDOW)[None, :]
    o = sink_attention(qb, band(k), band(v), qpos, kpos, sinks)
    out = o.reshape(b, t, ATTN_HEADS * ATTN_HEAD_DIM) @ w_o
    return out, k[:, t - WINDOW:], v[:, t - WINDOW:]

def swa_sample(x, k_buf, v_buf, w_qkv, sinks, w_o):
    b, t, _ = x.shape
    pos = PAST_LEN + jnp.arange(t)
    q, k, v = attn_project(x, w_qkv)
    q = rope(q, pos)
    k = rope(k, pos)
    kc = jnp.concatenate([k_buf.astype(k.dtype), k], axis=1)
    vc = jnp.concatenate([v_buf.astype(v.dtype), v], axis=1)
    kpos = PAST_LEN - WINDOW + jnp.arange(WINDOW + t)
    o = sink_attention(q, kc, vc, pos, kpos, sinks)
    out = o.reshape(b, t, ATTN_HEADS * ATTN_HEAD_DIM) @ w_o
    return out, kc[:, t:], vc[:, t:]

def retention_chunkwise(q, k, v, s0, chunk):
    b, t, h, dk = q.shape
    dv = v.shape[-1]
    nc = t // chunk
    log_gamma = jnp.log(1.0 - 2.0 ** (-5.0 - jnp.arange(RET_HEADS, dtype=jnp.float32)))
    idx = jnp.arange(chunk, dtype=jnp.float32)
    rel = idx[:, None] - idx[None, :]
    decay_in = jnp.where(rel[None] >= 0, jnp.exp(log_gamma[:, None, None] * jnp.maximum(rel, 0.0)[None]), 0.0)
    q_decay = jnp.exp(log_gamma[None, :] * (idx[:, None] + 1.0))
    k_decay = jnp.exp(log_gamma[None, :] * (chunk - 1.0 - idx[:, None]))
    chunk_decay = jnp.exp(log_gamma * chunk)
    qc = jnp.moveaxis(q.reshape(b, nc, chunk, h, dk), 1, 0)
    kc = jnp.moveaxis(k.reshape(b, nc, chunk, h, dk), 1, 0)
    vc = jnp.moveaxis(v.reshape(b, nc, chunk, h, dv), 1, 0)

    def step(s, inp):
        qi, ki, vi = inp
        inner = jnp.einsum('bihd,bjhd->bhij', qi, ki) * decay_in
        o = jnp.einsum('bhij,bjhe->bihe', inner, vi)
        o = o + jnp.einsum('bihd,bhde->bihe', qi, s) * q_decay[None, :, :, None]
        s = s * chunk_decay[None, :, None, None] + jnp.einsum('bjhd,bjhe->bhde', ki * k_decay[None, :, :, None], vi)
        return s, o

    s_new, o = lax.scan(step, s0, (qc, kc, vc))
    return jnp.moveaxis(o, 0, 1).reshape(b, t, h, dv), s_new

def retention_mixer(x, s0, pos, chunk, w_in, w_o):
    b, t, _ = x.shape
    hcat = x @ w_in
    nqk = RET_HEADS * RET_KEY_DIM
    nv = RET_HEADS * RET_VALUE_DIM
    q = hcat[..., :nqk].reshape(b, t, RET_HEADS, RET_KEY_DIM).astype(jnp.float32)
    k = hcat[..., nqk:2 * nqk].reshape(b, t, RET_HEADS, RET_KEY_DIM).astype(jnp.float32)
    v = hcat[..., 2 * nqk:2 * nqk + nv].reshape(b, t, RET_HEADS, RET_VALUE_DIM).astype(jnp.float32)
    g = hcat[..., 2 * nqk + nv:].astype(jnp.float32)
    q = retention_rotate(q, pos)
    k = retention_rotate(k, pos) * (RET_KEY_DIM ** -0.5)
    o, s_new = retention_chunkwise(q, k, v, s0.astype(jnp.float32), chunk)
    mu = jnp.mean(o, axis=-1, keepdims=True)
    var = jnp.mean(jnp.square(o - mu), axis=-1, keepdims=True)
    o = ((o - mu) * lax.rsqrt(var + GN_EPS)).reshape(b, t, nv)
    out = (jax.nn.silu(g) * o).astype(x.dtype) @ w_o
    return out, s_new

def conv_ffn(x, buf, w_in, conv_w, conv_b, w_out):
    t = x.shape[1]
    u = x @ w_in
    a, g = u[..., :D_FF], u[..., D_FF:]
    ext = jnp.concatenate([buf.astype(a.dtype), a], axis=1)
    c = conv_b + ext[:, 0:t] * conv_w[0]
    for j in range(1, CONV_WIDTH):
        c = c + ext[:, j:j + t] * conv_w[j]
    h = jax.nn.silu(c) * g
    return h @ w_out, ext[:, t:]

def setup_inputs(seed: int = 0) -> dict:
    key = jax.random.key(seed)
    ks = jax.random.split(key, 20)

    def nrm(k, shape, scale):
        return jax.random.normal(k, shape, jnp.float32) * scale

    qkv_dim = (ATTN_HEADS + 2 * ATTN_KV_HEADS) * ATTN_HEAD_DIM
    ret_in_dim = 2 * RET_HEADS * RET_KEY_DIM + 2 * RET_HEADS * RET_VALUE_DIM
    return {
        'x_prompt': nrm(ks[0], (BATCH, SEQ, D_MODEL), 1.0),
        'x_sample': nrm(ks[1], (DEC_BATCH, DEC_SEQ, D_MODEL), 1.0),
        'cache_k_win': nrm(ks[2], (N_ATTN_LAYERS, DEC_BATCH, WINDOW, ATTN_KV_HEADS, ATTN_HEAD_DIM), 1.0),
        'cache_v_win': nrm(ks[3], (N_ATTN_LAYERS, DEC_BATCH, WINDOW, ATTN_KV_HEADS, ATTN_HEAD_DIM), 1.0),
        'state_ret': nrm(ks[4], (N_RET_LAYERS, DEC_BATCH, RET_HEADS, RET_KEY_DIM, RET_VALUE_DIM), 0.1),
        'state_conv': nrm(ks[5], (DEPTH, DEC_BATCH, CONV_WIDTH - 1, D_FF), 1.0),
        'attn_w_qkv': nrm(ks[6], (N_ATTN_LAYERS, D_MODEL, qkv_dim), D_MODEL ** -0.5),
        'attn_sinks': nrm(ks[7], (N_ATTN_LAYERS, ATTN_HEADS), 0.5),
        'attn_w_o': nrm(ks[8], (N_ATTN_LAYERS, ATTN_HEADS * ATTN_HEAD_DIM, D_MODEL), DEEPNORM_BETA * (ATTN_HEADS * ATTN_HEAD_DIM) ** -0.5),
        'ret_w_in': nrm(ks[9], (N_RET_LAYERS, D_MODEL, ret_in_dim), D_MODEL ** -0.5),
        'ret_w_o': nrm(ks[10], (N_RET_LAYERS, RET_HEADS * RET_VALUE_DIM, D_MODEL), DEEPNORM_BETA * (RET_HEADS * RET_VALUE_DIM) ** -0.5),
        'ffn_w_in': nrm(ks[11], (DEPTH, D_MODEL, 2 * D_FF), D_MODEL ** -0.5),
        'ffn_conv_w': nrm(ks[12], (DEPTH, CONV_WIDTH, D_FF), CONV_WIDTH ** -0.5),
        'ffn_conv_b': nrm(ks[13], (DEPTH, D_FF), 0.02),
        'ffn_w_out': nrm(ks[14], (DEPTH, D_FF, D_MODEL), DEEPNORM_BETA * D_FF ** -0.5),
        'ln_mix_g': 1.0 + nrm(ks[15], (DEPTH, D_MODEL), 0.02),
        'ln_mix_b': nrm(ks[16], (DEPTH, D_MODEL), 0.02),
        'ln_ffn_g': 1.0 + nrm(ks[17], (DEPTH, D_MODEL), 0.02),
        'ln_ffn_b': nrm(ks[18], (DEPTH, D_MODEL), 0.02),
    }

def reference(x_prompt, x_sample, cache_k_win, cache_v_win, state_ret, state_conv,
              attn_w_qkv, attn_sinks, attn_w_o, ret_w_in, ret_w_o,
              ffn_w_in, ffn_conv_w, ffn_conv_b, ffn_w_out,
              ln_mix_g, ln_mix_b, ln_ffn_g, ln_ffn_b):
    xp, xs = x_prompt, x_sample
    bp, tp = xp.shape[0], xp.shape[1]
    ts = xs.shape[1]
    pos_p = jnp.arange(tp)
    pos_s = PAST_LEN + jnp.arange(ts)
    kp_l, vp_l, ks_l, vs_l, rp_l, rs_l, cp_l, cs_l = [], [], [], [], [], [], [], []
    for i in range(DEPTH):
        j = i // N_MIXERS
        if i % N_MIXERS == 0:
            mp, kp, vp = swa_prompt(xp, attn_w_qkv[j], attn_sinks[j], attn_w_o[j])
            ms, ksm, vsm = swa_sample(xs, cache_k_win[j], cache_v_win[j], attn_w_qkv[j], attn_sinks[j], attn_w_o[j])
            kp_l.append(kp)
            vp_l.append(vp)
            ks_l.append(ksm)
            vs_l.append(vsm)
        else:
            s0 = jnp.zeros((bp, RET_HEADS, RET_KEY_DIM, RET_VALUE_DIM), jnp.float32)
            mp, rp = retention_mixer(xp, s0, pos_p, RET_CHUNK, ret_w_in[j], ret_w_o[j])
            ms, rs = retention_mixer(xs, state_ret[j], pos_s, ts, ret_w_in[j], ret_w_o[j])
            rp_l.append(rp)
            rs_l.append(rs)
        xp = layer_norm(DEEPNORM_ALPHA * xp + mp, ln_mix_g[i], ln_mix_b[i])
        xs = layer_norm(DEEPNORM_ALPHA * xs + ms, ln_mix_g[i], ln_mix_b[i])
        buf0 = jnp.zeros((bp, CONV_WIDTH - 1, D_FF), xp.dtype)
        fp, cp = conv_ffn(xp, buf0, ffn_w_in[i], ffn_conv_w[i], ffn_conv_b[i], ffn_w_out[i])
        fs, cs = conv_ffn(xs, state_conv[i], ffn_w_in[i], ffn_conv_w[i], ffn_conv_b[i], ffn_w_out[i])
        cp_l.append(cp)
        cs_l.append(cs)
        xp = layer_norm(DEEPNORM_ALPHA * xp + fp, ln_ffn_g[i], ln_ffn_b[i])
        xs = layer_norm(DEEPNORM_ALPHA * xs + fs, ln_ffn_g[i], ln_ffn_b[i])
    return (xp, xs,
            jnp.stack(kp_l), jnp.stack(vp_l), jnp.stack(rp_l), jnp.stack(cp_l),
            jnp.stack(ks_l), jnp.stack(vs_l), jnp.stack(rs_l), jnp.stack(cs_l))


_drawn_inputs = setup_inputs


def setup_inputs(seed=0):
    import zlib

    import numpy as np

    out = dict(_drawn_inputs(seed))
    spreads = {}
    factors = {'attn_sinks': 46.471, 'ffn_conv_b': 8.0}
    for name, (base, spread) in spreads.items():
        noise = np.random.default_rng([zlib.crc32(name.encode()), seed]).standard_normal(out[name].shape)
        drawn = base * np.exp(spread * noise) if base else spread * noise
        out[name] = __import__('jax').numpy.asarray(drawn.astype(out[name].dtype))
    for name, factor in factors.items():
        out[name] = (out[name] * factor).astype(out[name].dtype)
    return out
```

```python
import numpy as np
import concourse.bass as bass
from concourse import mybir
from contextlib import ExitStack

F32 = mybir.dt.float32
F32R = mybir.dt.float32r
ALU = mybir.AluOpType
ACT = mybir.ActivationFunctionType
AXX = mybir.AxisListType.X

P = 128
D = 1024
SEQ = 1024
NS = 8
TOK = SEQ + NS
KT = D // P
NCH = 3
CH = TOK // NCH
HD = 64
NG = 4
GH = 4
W = 128
NB = SEQ // W
RH = 4
RK = 256
RV = 512
FF = 2816
FT = FF // P
NBLK = FT // 2
ALPHA = (2.0 * 2) ** 0.25
EPS = 1e-5
NEG = -1e30
LN_BIG = -3e38

SLAB = 1024
RING = 6
ATT_S = 5
ATT_N = NG * ATT_S
FFN_N = 6 * NBLK
S_ATT, S_FFN0 = 0, ATT_N
S_RIN = S_FFN0 + FFN_N
S_RO = S_RIN + 12 * RH
S_FFN1 = S_RO + 16
N_SLABS = S_FFN1 + FFN_N
AHEAD = 5


RAW = 3


def raw_slot(s):
    return s % ATT_S % RAW if s < ATT_N else (s - ATT_N) % RAW


def raw_use(s):
    return sum(raw_slot(n) == raw_slot(s) for n in range(s + 1))


def slot(s):
    return s % ATT_S if s < ATT_N else (s - ATT_N) % RING


UP_J, DOWN_J = 4 * NCH, KT * NCH
ATT_J = (NB + 1) + DOWN_J
FFN_J = NBLK * (UP_J + DOWN_J)
J_FFN0 = NG * ATT_J
J_RIN = J_FFN0 + FFN_J
J_RO = J_RIN + 12 * RH * NCH
J_FFN1 = J_RO + 8 * DOWN_J


def ended(s):
    if s < S_FFN0:
        g, j = divmod(s, ATT_S)
        return g * ATT_J + (NB + 1 if j < 3 else ATT_J)
    if s < S_RIN or s >= S_FFN1:
        j0, r = (J_FFN0, s - S_FFN0) if s < S_RIN else (J_FFN1, s - S_FFN1)
        if r < 4:
            return j0 + NCH * (r + 1)
        b, q = divmod(r - 4, 6)
        if b == NBLK - 1:
            return j0 + FFN_J
        return j0 + UP_J + b * (UP_J + DOWN_J) + (NCH * (q + 1) if q < 4 else UP_J + DOWN_J)
    if s < S_RO:
        return J_RIN + NCH * (s - S_RIN + 1)
    return J_RO + DOWN_J * ((s - S_RO) // 2 + 1)


ONE = 1
SEMS = {
    "": ("raw_in0 raw_in1 raw_in2 hi_done lo_done jobs x_in c_in x_hi x_lo x_y").split(),
    "a_": ("table_in cache_in proj rope_t v_hi v_fp v_free qk back t_hi t_lo score shifted small small2 expd "
             "inv probs pt pt_hi pt_lo heads heads_hi heads_lo yadd kv_out win_out s_sc s_scc s_row s_rowc "
             "s_tr s_mx s_nm s_ex s_inv s_p s_pt s_ptc s_dg s_o s_oh s_ol dchain passed").split(),
    "n_": "in_ mean centred squares var eps std inv scaled affine hi lo out".split(),
    "f0_": "in_ border a_in conv silu gate h_hi h_lo yadd out".split(),
    "f1_": "in_ border a_in conv silu gate h_hi h_lo yadd out".split(),
    "p_": "in_ prod rot plain out_r out_p0 out_p1".split(),
    "r_": ("in_ head_in qkvg0 qkvg1 turned q_hi q_lo k_hi k_lo v_hi v_lo gate inner inner_d inner_hi inner_lo out_ "
             "stats small root gated scaled back back_c o_out kv state s_hi s_lo s_out "
             "x_in x_turned x_rows x_mask st_in0 st_in1 decay spread outer x_o x_stats x_small x_root x_gated x_back x_backc "
             "x_out st_out0 st_out1 passed").split(),
    "o_": "in_ hi lo yadd".split(),
}

LN_COUNTS = {"in_": 32, "affine": KT * NCH, "out": 0} | dict.fromkeys(
    "mean centred squares var eps std inv scaled hi lo".split(), NCH)


def build(nc, A):
    ctx = ExitStack()
    with ctx:
        def sb(name, shape, dt=F32, c=ctx):
            return c.enter_context(nc.sbuf_tensor(name, shape, dt))

        sems = {p + n: ctx.enter_context(nc.semaphore(p + n)) for p, names in SEMS.items() for n in names}

        def sem(name):
            return sems[name]

        raw = sb("raw", [P, RAW, SLAB])
        wh = sb("wh", [P, RING, SLAB], F32R)
        wl = sb("wl", [P, RING, SLAB], F32R)
        xh = sb("xh", [P, KT, TOK], F32R)
        xl = sb("xl", [P, KT, TOK], F32R)
        y = sb("y", [P, KT, TOK])
        ident = sb("ident", [P, P])
        bank = [ctx.enter_context(nc.psum_tensor(f"bank{n}", [P, 512], F32)) for n in range(8)]

        raw_in = [sem(f"raw_in{n}") for n in range(RAW)]
        hi_done = sem("hi_done")
        lo_done = sem("lo_done")
        jobs = sem("jobs")

        def plus(i, per, base):
            return base if per == 0 else i * per + base

        def count(i, per, base):
            return plus(i, per, ONE + base)

        def load_slab(sp, s, i=0, n=0):
            if s >= 2:
                sp.wait_ge(lo_done, count(i, n, s - 1))
            src = A["w"][s] if n == 0 else A["w"][bass.ds(i * n + s, 1)].rearrange("a p n -> p (a n)")
            sp.dma_start(raw[:, raw_slot(s), :], src).then_inc(raw_in[raw_slot(s)], 16)

        def split_hi(act, s, i=0, n=0):
            if s >= N_SLABS or (isinstance(i, int) and s + i * n >= N_SLABS):
                return
            act.wait_ge(raw_in[raw_slot(s)], count(i, 16 * (raw_use(s + n) - raw_use(s)), 16 * raw_use(s)))
            if s >= AHEAD:
                act.wait_ge(jobs, count(i, ended(s - AHEAD + n) - ended(s - AHEAD), ended(s - AHEAD)))
            act.activation(wh[:, slot(s), :], raw[:, raw_slot(s), :], ACT.Copy).then_inc(hi_done, 1)

        def split_lo(dve, s, i=0, n=0):
            if s >= N_SLABS or (isinstance(i, int) and s + i * n >= N_SLABS):
                return
            dve.wait_ge(hi_done, count(i, n, s + 1))
            dve.tensor_tensor(wl[:, slot(s), :], raw[:, raw_slot(s), :], wh[:, slot(s), :].bitcast(F32),
                              ALU.subtract).then_inc(lo_done, 1)

        def columns(c):
            return slice(c * CH, (c + 1) * CH)

        def accumulate(pe, out, terms):
            n = len(terms)
            for k, (ah, al, bh, bl) in enumerate(terms):
                pe.matmul(out, ah, bh, start=(k == 0), stop=False)
                pe.matmul(out, ah, bl, start=False, stop=False)
                mm = pe.matmul(out, al, bh, start=False, stop=(k == n - 1))
            return mm

        def up_job(pe, out, s, c):
            def tile(w, k):
                return w[:, slot(s), k * P:(k + 1) * P]
            return accumulate(pe, out, [(tile(wh, k), tile(wl, k), xh[:, k, columns(c)], xl[:, k, columns(c)])
                                        for k in range(KT)])

        def down_job(pe, out, s, ft, c, mh, ml):
            def tile(w, k):
                return w[:, slot(s + k), ft * P:(ft + 1) * P]
            return accumulate(pe, out, [(tile(wh, k), tile(wl, k), mh[:, k, columns(c)], ml[:, k, columns(c)])
                                        for k in range(2)])

        x_in = sem("x_in")
        c_in = sem("c_in")
        x_hi = sem("x_hi")
        x_lo = sem("x_lo")
        x_y = sem("x_y")
        with nc.Block() as block:
            def set_one(eng, n):
                for name in list(sems)[n::5]:
                    eng.sem_inc(sems[name], ONE)

            @block.sync
            def _(sp):
                set_one(sp, 0)

            @block.scalar
            def _(act):
                set_one(act, 1)

            @block.vector
            def _(dve):
                set_one(dve, 2)

            @block.tensor
            def _(pe):
                set_one(pe, 3)

            @block.gpsimd
            def _(pool):
                set_one(pool, 4)

        with nc.Block() as block:
            @block.sync
            def _(sp):
                for s in range(AHEAD):
                    load_slab(sp, s)

            @block.scalar
            def _(act):
                act.dma_start(y[:, :, :], A["x"]).then_inc(x_in, 16)
                act.dma_start(ident[:, :], A["ident"]).then_inc(c_in, 16)
                act.wait_ge(x_in, ONE + 16)
                act.wait_ge(c_in, ONE + 16)
                act.activation(xh[:, :, :], y[:, :, :], ACT.Copy).then_inc(x_hi, 1)
                for s in range(AHEAD):
                    split_hi(act, s)
                act.wait_ge(x_lo, ONE + 1)
                act.activation(y[:, :, :], y[:, :, :], ACT.Copy, scale=ALPHA).then_inc(x_y, 1)

            @block.vector
            def _(dve):
                dve.wait_ge(x_hi, ONE + 1)
                dve.tensor_tensor(xl[:, :, :], y[:, :, :], xh[:, :, :].bitcast(F32),
                                  ALU.subtract).then_inc(x_lo, 1)
                for s in range(AHEAD):
                    split_lo(dve, s)

        S_ln = {n: sem("n_" + n) for n in LN_COUNTS}
        attention(nc, A, locals())
        layer_norm(nc, A, locals(), 0, "mix", True)
        conv_ffn(nc, A, locals(), 0)
        layer_norm(nc, A, locals(), 0, "ffn", True)
        retention_in(nc, A, locals())
        retention_core(nc, A, locals())
        retention_out(nc, A, locals())
        layer_norm(nc, A, locals(), 1, "mix", True)
        conv_ffn(nc, A, locals(), 1)
        layer_norm(nc, A, locals(), 1, "ffn", False)


def attention(nc, A, env):
    ctx, sem, bank, plus, count = env["ctx"], env["sem"], env["bank"], env["plus"], env["count"]
    xh, xl, y, wh, wl, ident = (env[n] for n in ("xh", "xl", "y", "wh", "wl", "ident"))
    jobs, lo_done = env["jobs"], env["lo_done"]
    load_slab, split_hi, split_lo = env["load_slab"], env["split_hi"], env["split_lo"]
    columns, accumulate, down_job = env["columns"], env["accumulate"], env["down_job"]
    S = {n: sem("a_" + n) for n in SEMS["a_"]}
    KR, VR = 4, 5

    with ExitStack() as c:
        def sb(name, shape, dt=F32):
            return c.enter_context(nc.sbuf_tensor("a_" + name, shape, dt))
        cosT = sb("cosT", [P, NB + 1, 32])
        sinT = sb("sinT", [P, NB + 1, 32])
        mask = sb("mask", [P, 2 * W])
        sinkb = sb("sinkb", [P, NG * GH])
        sinkc = sb("sinkc", [32, NG])
        same = sb("same", [32, NS])
        t1 = sb("t1", [P, 2, 320])
        t2 = sb("t2", [P, 2, 320])
        qk = sb("qk", [P, 2, 384])
        vh = sb("vh", [P, VR, 2, HD], F32R)
        vl = sb("vl", [P, VR, 2, HD], F32R)
        vf = sb("vf", [P, 2, HD])
        vs2 = sb("vs2", [NS, 2, HD])
        qh = sb("qh", [P, 256], F32R)
        ql = sb("ql", [P, 256], F32R)
        kh = sb("kh", [P, KR * W], F32R)
        kl = sb("kl", [P, KR * W], F32R)
        sm = sb("sm", [P, GH, 2 * W])
        prob = sb("prob", [P, GH, 2 * W])
        st = sb("st", [P, 8, GH])
        pth = sb("pth", [P, 2, GH * W], F32R)
        ptl = sb("ptl", [P, 2, GH * W], F32R)
        oh = sb("oh", [P, 2, TOK], F32R)
        ol = sb("ol", [P, 2, TOK], F32R)
        sq = sb("sq", [P, 3, NS])
        kc = sb("kc", [P, NS, W])
        vc = sb("vc", [P, NS, 2, HD])
        ss = sb("ss", [P, 32])
        row = sb("row", [1, 32])
        sp_ = sb("sp", [32, W + 1])
        sst = sb("sst", [32, 8])
        spt = sb("spt", [P, 32])
        dg = sb("dg", [32, 32])
        pn = sb("pn", [NS, 32])

        with nc.Block() as block:
            @block.sync
            def _(sp):
                for n, t in (("cosT", cosT), ("sinT", sinT), ("mask", mask), ("sinkb", sinkb), ("sinkc", sinkc), ("same", same)):
                    sp.dma_start(t[tuple([slice(None)] * len(t.shape))], A[n]).then_inc(S["table_in"], 16)
                with sp.Fori(0, NG) as g:
                    sp.wait_ge(S["s_o"], ONE + g)
                    kcg = A["kcache"][bass.ds(g, 1)].rearrange("a d b k -> d (a b) k")
                    sp.dma_start(kc[0:HD, :, :], kcg).then_inc(S["cache_in"], 16)
                    sp.dma_start(kc[HD:P, :, :], kcg).then_inc(S["cache_in"], 16)
                    vcg = A["vcache"][bass.ds(g, 1)].rearrange("a k b d -> k (a b) d")
                    sp.dma_start(vc[:, :, 0, :], vcg).then_inc(S["cache_in"], 16)
                    sp.dma_start(vc[:, :, 1, :], vcg).then_inc(S["cache_in"], 16)
                    for j in range(ATT_S):
                        load_slab(sp, AHEAD + j, g, ATT_S)
                sp.dma_start(A["kwin_s"][:, 0:W - 1, :, :], A["kcache_rows"][:, 1:W, :, :]).then_inc(S["win_out"], 16)
                sp.dma_start(A["vwin_s"][:, 0:W - 1, :, :], A["vcache_rows"][:, 1:W, :, :]).then_inc(S["win_out"], 16)
                sp.wait_ge(S["win_out"], ONE + 32)

            @block.tensor
            def _(pe):
                pe.wait_ge(S["table_in"], ONE + 16 * 6)
                with pe.Fori(0, NG) as g:
                    def project(b):
                        m = P if b < NB else NS
                        if b == 0:
                            pe.wait_ge(lo_done, count(g, ATT_S, 3))
                            pe.wait_ge(S["yadd"], count(g, DOWN_J, 0))
                        if b >= 2:
                            pe.wait_ge(S["v_free"], count(g, NB, b - 1))
                        o = bank[b % 2][0:m, 0:384].rearrange("m (a n) -> m a n", a=3)
                        terms = []
                        for k in range(KT):
                            t = slice(b * W, b * W + m)
                            kk = slice(k * P, (k + 1) * P)
                            terms.append((xh[:, k, t], xl[:, k, t], wh[:, 0:3, kk], wl[:, 0:3, kk]))
                        accumulate(pe, o, terms).then_inc(jobs, 1)

                    def turn(b):
                        m = P if b < NB else NS
                        pe.wait_ge(S["qk"], count(g, 2 * (NB + 1), 2 * b + 2))
                        if b >= 1:
                            pe.wait_ge(S["t_lo"], count(g, 2 * NB + 1, 2 * b))
                        pe.sem_inc(S["passed"], 1)
                        for j in range(3):
                            t = pe.transpose(bank[2][:, j * P:j * P + m], qk[0:m, b % 2, j * P:(j + 1) * P],
                                             ident[0:m, 0:m])
                        t.then_inc(S["back"], 1)

                    def scores(b):
                        pe.wait_ge(S["t_lo"], count(g, 2 * NB + 1, 2 * b + 2))
                        if b >= 1:
                            pe.wait_ge(S["shifted"], count(g, GH * NB, GH * b))
                        kb = b % KR * W
                        pieces = [(kb, W, W)] if b == 0 else [(kb - W, 0, 2 * W)] if b % KR else [((KR - 1) * W, 0, W), (0, W, W)]
                        for h in range(GH):
                            r = slice(HD * (h % 2), HD * (h % 2) + HD)
                            q = slice(W * (h // 2), W * (h // 2) + W)
                            for k0, at, n in pieces:
                                o = bank[3 + h % 2][:, (h // 2) * 256 + at:(h // 2) * 256 + at + n]
                                mm = accumulate(pe, o, [(qh[r, q], ql[r, q], kh[r, k0:k0 + n], kl[r, k0:k0 + n])])
                        mm.then_inc(S["score"], 1)

                    def turn_probs(b):
                        pe.wait_ge(S["probs"], count(g, NB, b + 1))
                        if b >= 1:
                            pe.wait_ge(S["pt_lo"], count(g, NB, b))
                        for t in range(0 if b else 1, 2):
                            for h in range(GH):
                                mm = pe.transpose(bank[5 + t][:, h * W:(h + 1) * W], prob[:, h, t * W:(t + 1) * W],
                                                  ident[:, :])
                        mm.then_inc(S["pt"], 1)

                    def values(b):
                        pe.wait_ge(S["pt_lo"], count(g, NB, b + 1))
                        if b >= 1:
                            pe.wait_ge(S["heads_lo"], count(g, NB, b))
                        terms = []
                        for t in range(0 if b else 1, 2):
                            v = b - 1 + t
                            terms.append((vh[:, v % VR, :, :], vl[:, v % VR, :, :], pth[:, t, :], ptl[:, t, :]))
                        accumulate(pe, bank[7][:, :], terms).then_inc(S["heads"], 1)

                    for t in range(NB + 3):
                        if t <= NB:
                            project(t)
                        if 1 <= t <= NB + 1:
                            turn(t - 1)
                        if 1 <= t <= NB:
                            scores(t - 1)
                        if 2 <= t <= NB + 1:
                            turn_probs(t - 2)
                        if 3 <= t <= NB + 2:
                            values(t - 3)

                    pe.wait_ge(S["t_lo"], count(g, 2 * NB + 1, 2 * NB + 1))
                    pe.wait_ge(S["cache_in"], count(g, 64, 64))
                    for b in range(NS):
                        for h in range(2):
                            r = slice(HD * h, HD * h + HD)
                            pe.matmul(bank[h][:, b * 4 + h:b * 4 + 4:2], kc[r, b, :], sq[r, 0:2, b],
                                      start=True, stop=True)
                    for b in range(NS):
                        for h in range(2):
                            r = slice(HD * h, HD * h + HD)
                            mm = pe.matmul(bank[3 + h][0:1, b * 4 + h:b * 4 + 4:2], sq[r, 2, b:b + 1], sq[r, 0:2, b],
                                           start=True, stop=True)
                    mm.then_inc(S["s_sc"], 1)
                    pe.wait_ge(S["s_scc"], ONE + 4 * g + 4)
                    pe.sem_inc(S["passed"], 1)
                    pe.transpose(bank[2][0:32, 0:W], ss[:, :], ident[:, :])
                    pe.matmul(bank[2][0:32, W:W + 1], row[:, :], ident[0:1, 0:1], start=True,
                              stop=True).then_inc(S["s_tr"], 1)
                    pe.wait_ge(S["dchain"], count(g, 4, 4))
                    pe.wait_ge(S["s_p"], ONE + g + 1)
                    pe.sem_inc(S["passed"], 1)
                    pe.transpose(bank[0][:, 0:32], sp_[:, 0:W], ident[0:32, 0:32])
                    pe.matmul(bank[1][0:NS, 0:32], same[:, :], dg[:, :], start=True, stop=True).then_inc(S["s_pt"], 1)
                    pe.wait_ge(S["s_ptc"], ONE + 2 * g + 2)
                    for b in range(NS):
                        o = bank[2][:, b * 4:b * 4 + 4]
                        pe.matmul(o, vc[:, b, :, :], spt[:, b * 4:b * 4 + 4], start=True, stop=False)
                        mm = pe.matmul(o, vs2[:, :, :], pn[:, b * 4:b * 4 + 4], start=False, stop=True)
                    mm.then_inc(S["s_o"], 1)

                    pe.wait_ge(S["heads_lo"], count(g, NB, NB))
                    pe.wait_ge(S["s_ol"], ONE + 2 * g + 2)
                    pe.wait_ge(lo_done, count(g, ATT_S, ATT_S))
                    for ft in range(KT):
                        for ch in range(NCH):
                            q = ft * NCH + ch
                            if q >= 4:
                                pe.wait_ge(S["yadd"], count(g, DOWN_J, q - 3))
                            down_job(pe, bank[q % 4][:, 0:CH], 3, ft, ch, oh, ol).then_inc(jobs, 1)

            @block.scalar
            def _(act):
                act.wait_ge(S["table_in"], ONE + 16 * 6)
                with act.Fori(0, NG) as g:
                    def v_hi(b):
                        m = P if b < NB else NS
                        act.wait_ge(jobs, count(g, ATT_J, b + 1))
                        if b < NB:
                            act.wait_ge(S["heads"], count(g, NB, max(b - 3, 0)))
                            act.activation(vh[:, b % VR, :, :], bank[b % 2][:, 320:384].rearrange("m (a n) -> m a n", a=1)
                                           .to_broadcast([P, 2, HD]), ACT.Copy).then_inc(S["v_hi"], 1)
                        if b == NB - 1:
                            act.wait_ge(S["kv_out"], count(g, 64, 0))
                            act.activation(vf[:, 0, :], bank[b % 2][:, 320:384], ACT.Copy).then_inc(S["v_fp"], 1)
                        if b == NB:
                            act.wait_ge(S["s_o"], ONE + g)
                            act.activation(vs2[:, :, :], bank[b % 2][0:NS, 320:384].rearrange("m (a n) -> m a n", a=1)
                                           .to_broadcast([NS, 2, HD]), ACT.Copy).then_inc(S["v_fp"], 1)

                    def t_hi(b):
                        act.wait_ge(S["back"], count(g, NB + 1, b + 1))
                        if b < NB:
                            act.wait_ge(S["score"], count(g, NB, b))
                            act.activation(qh[:, :], bank[2][:, 0:256], ACT.Copy).then_inc(S["t_hi"], 1)
                            act.activation(kh[:, b % KR * W:(b % KR + 1) * W], bank[2][:, 256:384], ACT.Copy).then_inc(S["t_hi"], 1)

                    def exps(b):
                        act.wait_ge(S["small"], count(g, 3 * NB, 3 * b + 3))
                        k0 = 0 if b else W
                        act.wait_ge(S["pt"], count(g, NB, b))
                        for h in range(GH):
                            act.activation(prob[:, h, k0:], sm[:, h, k0:], ACT.Exp, bias=st[:, 2, h:h + 1],
                                           accum_out=st[:, 4, h:h + 1])
                        act.activation(st[:, 5, :], st[:, 3, :], ACT.Exp).then_inc(S["expd"], 1)

                    def pt_hi(b):
                        act.wait_ge(S["pt"], count(g, NB, b + 1))
                        act.wait_ge(S["heads"], count(g, NB, b))
                        for t in range(0 if b else 1, 2):
                            a = act.activation(pth[:, t, :], bank[5 + t][:, :], ACT.Copy)
                        a.then_inc(S["pt_hi"], 1)

                    def heads_hi(b):
                        act.wait_ge(S["heads"], count(g, NB, b + 1))
                        if b == 0:
                            act.wait_ge(jobs, count(g, ATT_J, 0))
                        for h in range(2):
                            r = slice(HD * h, HD * h + HD)
                            a = act.activation(oh[r, :, b * W:(b + 1) * W],
                                               bank[7][r, :].rearrange("p (j h n) -> p j h n", j=2, h=2)[:, :, h, :],
                                               ACT.Copy)
                        a.then_inc(S["heads_hi"], 1)

                    for t in range(NB + 3):
                        if t <= NB:
                            v_hi(t)
                        if 1 <= t <= NB + 1:
                            t_hi(t - 1)
                        if 2 <= t <= NB + 1:
                            exps(t - 2)
                            pt_hi(t - 2)
                        if 3 <= t <= NB + 2:
                            heads_hi(t - 3)
                    for j in range(3):
                        split_hi(act, ATT_S + j, g, ATT_S)

                    act.wait_ge(S["qk"], count(g, 2 * (NB + 1), 2 * (NB + 1)))
                    act.wait_ge(S["v_fp"], ONE + 2 * g + 2)
                    gg = bass.ds(g, 1)
                    act.dma_start(A["kwin_p"][:, gg, :].rearrange("t a d -> t (a d)"), qk[:, 1, 256:320]).then_inc(S["kv_out"], 16)
                    act.dma_start(A["vwin_p"][:, gg, :].rearrange("t a d -> t (a d)"), vf[:, 0, :]).then_inc(S["kv_out"], 16)
                    act.dma_start(A["kwin_s"][:, W - 1, gg, :].rearrange("t a d -> t (a d)"), qk[0:NS, 0, 256:320]).then_inc(S["kv_out"], 16)
                    act.dma_start(A["vwin_s"][:, W - 1, gg, :].rearrange("t a d -> t (a d)"), vs2[:, 0, :]).then_inc(S["kv_out"], 16)

                    act.wait_ge(S["s_mx"], ONE + 3 * g + 3)
                    act.activation(sp_[:, :], bank[2][0:32, 0:W + 1], ACT.Exp, bias=sst[:, 2:3], scale=HD ** -0.5,
                                   accum_out=sst[:, 4:5])
                    act.activation(sst[:, 5:6], sst[:, 3:4], ACT.Exp).then_inc(S["s_ex"], 1)
                    act.wait_ge(S["s_o"], ONE + g + 1)
                    for h in range(2):
                        r = slice(HD * h, HD * h + HD)
                        act.activation(oh[r, :, SEQ:TOK],
                                       bank[2][r, 0:32].rearrange("p (b j h) -> p j h b", j=2, h=2)[:, :, h, :],
                                       ACT.Copy).then_inc(S["s_oh"], 1)
                    act.wait_ge(jobs, count(g, ATT_J, ATT_J))
                    for j in range(3, ATT_S):
                        split_hi(act, ATT_S + j, g, ATT_S)
                act.wait_ge(S["kv_out"], ONE + 64 * NG)

            @block.vector
            def _(dve):
                dve.wait_ge(S["table_in"], ONE + 16 * 6)
                with dve.Fori(0, NG) as g:
                    def rope(b):
                        m = P if b < NB else NS
                        if b < NB:
                            dve.wait_ge(S["v_hi"], count(g, NB, b + 1))
                        if b >= NB - 1:
                            dve.wait_ge(S["v_fp"], count(g, 2, b - NB + 2))
                        dve.wait_ge(S["qk"], count(g, 2 * (NB + 1), 2 * (b - 1)) if b >= 2 else count(g, 2 * (NB + 1), 0))
                        src = bank[b % 2][0:m, 0:320].rearrange("m (h a n) -> m h a n", h=5, a=2)
                        a1 = t1[0:m, b % 2, :].rearrange("m (h a n) -> m h a n", h=5, a=2)
                        a2 = t2[0:m, b % 2, :].rearrange("m (h a n) -> m h a n", h=5, a=2)
                        cs = cosT[0:m, b:b + 1, :].rearrange("m (a c) n -> m a c n", a=1)
                        sn = sinT[0:m, b, :].rearrange("m (a n) -> m a n", a=1)
                        dve.tensor_tensor(a1, src, cs.to_broadcast([m, 5, 2, 32]), ALU.mult)
                        dve.tensor_tensor(a2[:, :, 1, :], src[:, :, 0, :], sn.to_broadcast([m, 5, 32]), ALU.mult)
                        dve.scalar_tensor_tensor(a2[:, :, 0, :], src[:, :, 1, :], -1.0, sn.to_broadcast([m, 5, 32]),
                                                 ALU.mult, ALU.mult).then_inc(S["rope_t"], 1)
                        if b < NB:
                            dve.tensor_tensor(vl[:, b % VR, :, :], bank[b % 2][:, 320:384].rearrange("m (a n) -> m a n", a=1)
                                              .to_broadcast([P, 2, HD]), vh[:, b % VR, :, :].bitcast(F32),
                                              ALU.subtract).then_inc(S["v_free"], 1)

                    def t_lo(b):
                        if b < NB:
                            dve.wait_ge(S["t_hi"], count(g, 2 * NB, 2 * b + 2))
                            dve.tensor_tensor(ql[:, :], bank[2][:, 0:256], qh[:, :].bitcast(F32), ALU.subtract).then_inc(S["t_lo"], 1)
                            dve.tensor_tensor(kl[:, b % KR * W:(b % KR + 1) * W], bank[2][:, 256:384],
                                              kh[:, b % KR * W:(b % KR + 1) * W].bitcast(F32), ALU.subtract).then_inc(S["t_lo"], 1)
                        else:
                            dve.wait_ge(S["back"], count(g, NB + 1, NB + 1))
                            dve.tensor_copy(sq[:, :, :], bank[2][:, 0:384].rearrange("p (a n) -> p a n", a=3)[:, :, 0:NS])\
                               .then_inc(S["t_lo"], 1)

                    def shift(b):
                        dve.wait_ge(S["score"], count(g, NB, b + 1))
                        dve.wait_ge(S["expd"], count(g, NB, b))
                        k0 = 0 if b else W
                        dve.sem_inc(S["passed"], 1)
                        for h in range(GH):
                            dve.tensor_tensor_reduce(out=sm[:, h, k0:], in0=bank[3 + h % 2][:, (h // 2) * 256 + k0:(h // 2) * 256 + 256],
                                                     in1=mask[:, k0:], scale=HD ** -0.5, scalar=LN_BIG, op0=ALU.add,
                                                     op1=ALU.max, accum_out=st[:, 0, h:h + 1]).then_inc(S["shifted"], 1)
                        dve.wait_ge(S["shifted"], count(g, GH * NB, GH * b + GH))
                        sk = sinkb[:, bass.ds(g * GH, GH)]
                        dve.tensor_tensor(st[:, 1, :], st[:, 0, :], sk, ALU.max).then_inc(S["small"], 1)
                        dve.wait_ge(S["small"], count(g, 3 * NB, 3 * b + 1))
                        dve.tensor_scalar(st[:, 2, :], st[:, 1, :], -1.0, None, ALU.mult).then_inc(S["small"], 1)
                        dve.tensor_tensor(st[:, 3, :], sk, st[:, 1, :], ALU.subtract).then_inc(S["small"], 1)

                    def inverse(b):
                        dve.wait_ge(S["expd"], count(g, NB, b + 1))
                        dve.wait_ge(S["probs"], count(g, NB, b))
                        dve.tensor_tensor(st[:, 6, :], st[:, 4, :], st[:, 5, :], ALU.add).then_inc(S["small2"], 1)
                        dve.wait_ge(S["small2"], count(g, NB, b + 1))
                        dve.reciprocal(st[:, 7, :], st[:, 6, :]).then_inc(S["inv"], 1)

                    def pt_lo(b):
                        dve.wait_ge(S["pt_hi"], count(g, NB, b + 1))
                        for t in range(0 if b else 1, 2):
                            a = dve.tensor_tensor(ptl[:, t, :], bank[5 + t][:, :], pth[:, t, :].bitcast(F32), ALU.subtract)
                        a.then_inc(S["pt_lo"], 1)

                    def heads_lo(b):
                        dve.wait_ge(S["heads_hi"], count(g, NB, b + 1))
                        for h in range(2):
                            r = slice(HD * h, HD * h + HD)
                            a = dve.tensor_tensor(ol[r, :, b * W:(b + 1) * W],
                                                  bank[7][r, :].rearrange("p (j h n) -> p j h n", j=2, h=2)[:, :, h, :],
                                                  oh[r, :, b * W:(b + 1) * W].bitcast(F32), ALU.subtract)
                        a.then_inc(S["heads_lo"], 1)

                    for t in range(NB + 3):
                        if t <= NB:
                            rope(t)
                        if 1 <= t <= NB + 1:
                            t_lo(t - 1)
                        if 2 <= t <= NB + 1:
                            inverse(t - 2)
                            pt_lo(t - 2)
                        if 1 <= t <= NB:
                            shift(t - 1)
                        if 3 <= t <= NB + 2:
                            heads_lo(t - 3)
                    for j in range(3):
                        split_lo(dve, ATT_S + j, g, ATT_S)

                    dve.wait_ge(S["s_sc"], ONE + g + 1)
                    for n in range(2):
                        dve.tensor_copy(ss[:, n:32:2], bank[n][:, n:32:2]).then_inc(S["s_scc"], 1)
                        dve.tensor_copy(row[:, n:32:2], bank[3 + n][0:1, n:32:2]).then_inc(S["s_scc"], 1)
                    dve.wait_ge(S["s_tr"], ONE + g + 1)
                    dve.reduce_max(sst[:, 0:1], bank[2][0:32, 0:W + 1], AXX).then_inc(S["dchain"], 1)
                    dve.wait_ge(S["dchain"], count(g, 4, 1))
                    skc = sinkc[:, bass.ds(g, 1)]
                    dve.tensor_scalar(sst[:, 1:2], sst[:, 0:1], HD ** -0.5, skc, ALU.mult, ALU.max).then_inc(S["s_mx"], 1)
                    dve.wait_ge(S["s_mx"], count(g, 3, 1))
                    dve.tensor_scalar(sst[:, 2:3], sst[:, 1:2], -1.0, None, ALU.mult).then_inc(S["s_mx"], 1)
                    dve.tensor_tensor(sst[:, 3:4], skc, sst[:, 1:2], ALU.subtract).then_inc(S["s_mx"], 1)
                    dve.wait_ge(S["s_ex"], ONE + g + 1)
                    dve.tensor_tensor(sst[:, 6:7], sst[:, 4:5], sst[:, 5:6], ALU.add).then_inc(S["dchain"], 1)
                    dve.wait_ge(S["dchain"], count(g, 4, 2))
                    dve.reciprocal(sst[:, 7:8], sst[:, 6:7]).then_inc(S["dchain"], 1)
                    dve.wait_ge(S["dchain"], count(g, 4, 3))
                    dve.tensor_scalar(sp_[:, :], sp_[:, :], sst[:, 7:8], None, ALU.mult).then_inc(S["dchain"], 1)
                    dve.wait_ge(S["dchain"], count(g, 4, 4))
                    dve.tensor_scalar(dg[:, :], ident[0:32, 0:32], sp_[:, W:W + 1], None, ALU.mult).then_inc(S["s_p"], 1)
                    dve.wait_ge(S["s_pt"], ONE + g + 1)
                    dve.tensor_copy(spt[:, :], bank[0][:, 0:32]).then_inc(S["s_ptc"], 1)
                    dve.tensor_copy(pn[:, :], bank[1][0:NS, 0:32]).then_inc(S["s_ptc"], 1)
                    dve.wait_ge(S["s_oh"], ONE + 2 * g + 2)
                    for h in range(2):
                        r = slice(HD * h, HD * h + HD)
                        dve.tensor_tensor(ol[r, :, SEQ:TOK],
                                          bank[2][r, 0:32].rearrange("p (b j h) -> p j h b", j=2, h=2)[:, :, h, :],
                                          oh[r, :, SEQ:TOK].bitcast(F32), ALU.subtract).then_inc(S["s_ol"], 1)
                    for q in range(DOWN_J):
                        ft, ch = divmod(q, NCH)
                        dve.wait_ge(jobs, count(g, ATT_J, NB + 2 + q))
                        dve.tensor_tensor(y[:, ft, columns(ch)], bank[q % 4][:, 0:CH], y[:, ft, columns(ch)],
                                          ALU.add).then_inc(S["yadd"], 1)
                    for j in range(3, ATT_S):
                        split_lo(dve, ATT_S + j, g, ATT_S)

            @block.gpsimd
            def _(pool):
                with pool.Fori(0, NG) as g:
                    def add_rope(b):
                        m = P if b < NB else NS
                        pool.wait_ge(S["rope_t"], count(g, NB + 1, b + 1))
                        pool.wait_ge(S["back"], count(g, NB + 1, max(b - 1, 0)))
                        if b == 0 or b == 1:
                            pool.wait_ge(S["kv_out"], count(g, 64, 0))
                        pool.tensor_tensor(qk[0:m, b % 2, 0:256], t1[0:m, b % 2, 0:256], t2[0:m, b % 2, 0:256],
                                           ALU.add).then_inc(S["qk"], 1)
                        def twice(t):
                            return t[0:m, b % 2, 256:320].rearrange("m (a n) -> m a n", a=1).to_broadcast([m, 2, HD])
                        pool.tensor_tensor(qk[0:m, b % 2, 256:384].rearrange("m (a n) -> m a n", a=2), twice(t1), twice(t2),
                                           ALU.add).then_inc(S["qk"], 1)

                    def probs(b):
                        pool.wait_ge(S["inv"], count(g, NB, b + 1))
                        k0 = 0 if b else W
                        pool.tensor_tensor(prob[:, :, k0:], prob[:, :, k0:],
                                           st[:, 7, :].rearrange("p (h a) -> p h a", a=1).to_broadcast([P, GH, 2 * W - k0]),
                                           ALU.mult).then_inc(S["probs"], 1)

                    for t in range(NB + 2):
                        if t <= NB:
                            add_rope(t)
                        if t >= 2:
                            probs(t - 2)


def layer_norm(nc, A, env, layer, which, more):
    ctx, sem, bank = env["ctx"], env["sem"], env["bank"]
    xh, xl, y, columns = env["xh"], env["xl"], env["y"], env["columns"]
    nm = f"n{layer}{which}_"
    S = env["S_ln"]
    past = {n: (2 * layer + (which == "ffn")) * k for n, k in LN_COUNTS.items()}
    with ExitStack() as c:
        def sb(name, shape, dt=F32):
            return c.enter_context(nc.sbuf_tensor(nm + name, shape, dt))
        ones = sb("ones", [P, P])
        gb = sb("gb", [P, 2, KT])
        sq = sb("sq", [P, KT, CH])
        rs = sb("rs", [P, NCH, CH])

        with nc.Block() as block:
            @block.sync
            def _(sp):
                sp.dma_start(gb[:, :, :], A[f"ln_{which}"][layer]).then_inc(S["in_"], 16)
                sp.dma_start(ones[:, :], A["ones"]).then_inc(S["in_"], 16)
                if not more:
                    for ch in range(NCH):
                        sp.wait_ge(S["affine"], ONE + KT * (ch + 1) + past["affine"])
                        sp.dma_start(A["y"][:, :, columns(ch)], y[:, :, columns(ch)]).then_inc(S["out"], 16)
                    sp.wait_ge(S["out"], ONE + 16 * NCH + past["out"])

            @block.tensor
            def _(pe):
                pe.wait_ge(S["in_"], ONE + 32 + past["in_"])

                def mean(ch):
                    for k in range(KT):
                        mm = pe.matmul(bank[ch][:, 0:CH], ones[:, :], y[:, k, columns(ch)], start=(k == 0), stop=(k == KT - 1))
                    mm.then_inc(S["mean"], 1)

                def var(ch):
                    pe.wait_ge(S["squares"], ONE + ch + 1 + past["squares"])
                    for k in range(KT):
                        mm = pe.matmul(bank[3 + ch][:, 0:CH], ones[:, :], sq[:, k, :], start=(k == 0), stop=(k == KT - 1))
                    mm.then_inc(S["var"], 1)

                for ch in range(NCH):
                    mean(ch)
                for ch in range(NCH):
                    var(ch)

            @block.scalar
            def _(act):
                act.wait_ge(S["in_"], ONE + 32 + past["in_"])
                for ch in range(NCH):
                    act.wait_ge(S["centred"], ONE + ch + 1 + past["centred"])
                    if ch >= 1:
                        act.wait_ge(S["var"], ONE + ch + past["var"])
                    act.activation(sq[:, :, :], y[:, :, columns(ch)], ACT.Square).then_inc(S["squares"], 1)
                    act.wait_ge(S["eps"], ONE + ch + 1 + past["eps"])
                    act.activation(rs[:, ch, :], rs[:, ch, :], ACT.Sqrt).then_inc(S["std"], 1)
                if more:
                    for ch in range(NCH):
                        act.wait_ge(S["affine"], ONE + KT * (ch + 1) + past["affine"])
                        act.activation(xh[:, :, columns(ch)], y[:, :, columns(ch)], ACT.Copy).then_inc(S["hi"], 1)
                        act.wait_ge(S["lo"], ONE + ch + 1 + past["lo"])
                        act.activation(y[:, :, columns(ch)], y[:, :, columns(ch)], ACT.Copy, scale=ALPHA)

            @block.vector
            def _(dve):
                dve.wait_ge(S["in_"], ONE + 32 + past["in_"])

                def every(t):
                    return t.rearrange("p (a n) -> p a n", a=1).to_broadcast([P, KT, CH])

                def centre(ch):
                    dve.wait_ge(S["mean"], ONE + ch + 1 + past["mean"])
                    dve.tensor_tensor(y[:, :, columns(ch)], y[:, :, columns(ch)], every(bank[ch][:, 0:CH]),
                                      ALU.subtract).then_inc(S["centred"], 1)

                def scale(ch):
                    dve.wait_ge(S["var"], ONE + ch + 1 + past["var"])
                    dve.tensor_scalar(rs[:, ch, :], bank[3 + ch][:, 0:CH], EPS, None, ALU.add).then_inc(S["eps"], 1)
                    dve.wait_ge(S["std"], ONE + ch + 1 + past["std"])
                    dve.reciprocal(rs[:, ch, :], rs[:, ch, :]).then_inc(S["inv"], 1)
                    dve.wait_ge(S["inv"], ONE + ch + 1 + past["inv"])
                    dve.tensor_tensor(y[:, :, columns(ch)], y[:, :, columns(ch)], every(rs[:, ch, :]),
                                      ALU.mult).then_inc(S["scaled"], 1)
                    dve.wait_ge(S["scaled"], ONE + ch + 1 + past["scaled"])
                    for k in range(KT):
                        dve.tensor_scalar(y[:, k, columns(ch)], y[:, k, columns(ch)], gb[:, 0, k:k + 1], gb[:, 1, k:k + 1],
                                          ALU.mult, ALU.add).then_inc(S["affine"], 1)

                centre(0)
                centre(1)
                scale(0)
                centre(2)
                scale(1)
                scale(2)

            @block.gpsimd
            def _(pool):
                if more:
                    for ch in range(NCH):
                        pool.wait_ge(S["hi"], ONE + ch + 1 + past["hi"])
                        pool.tensor_tensor(xl[:, :, columns(ch)], y[:, :, columns(ch)],
                                           xh[:, :, columns(ch)].bitcast(F32), ALU.subtract).then_inc(S["lo"], 1)


def conv_ffn(nc, A, env, layer):
    ctx, sem, bank, plus, count = env["ctx"], env["sem"], env["bank"], env["plus"], env["count"]
    y = env["y"]
    jobs, lo_done = env["jobs"], env["lo_done"]
    load_slab, split_hi, split_lo = env["load_slab"], env["split_hi"], env["split_lo"]
    columns, up_job, down_job = env["columns"], env["up_job"], env["down_job"]
    s0, j0 = (S_FFN0, J_FFN0) if layer == 0 else (S_FFN1, J_FFN1)
    nm = f"f{layer}_"
    S = {n: sem(nm + n) for n in SEMS[nm]}
    IT = UP_J + DOWN_J
    LOOPS = (NBLK - 1) // 2 - layer

    with ExitStack() as c:
        def sb(name, shape, dt=F32):
            return c.enter_context(nc.sbuf_tensor(nm + name, shape, dt))
        ab = sb("ab", [P, TOK + 2])
        cv = sb("cv", [P, TOK])
        hf = sb("hf", [P, TOK])
        hh = sb("hh", [P, 2, 2, TOK], F32R)
        hl = sb("hl", [P, 2, 2, TOK], F32R)
        taps = sb("taps", [P, FT * 4])
        past = sb("past", [P, FT, 2, NS])
        cout = sb("cout", [P, FT * 10])

        with nc.Block() as block:
            @block.sync
            def _(sp):
                sp.dma_start(taps[:, :], A["taps"][layer]).then_inc(S["in_"], 16)
                sp.dma_start(past[:, :, :, :], A["past"][layer]).then_inc(S["in_"], 16)
                first = s0 + AHEAD
                n = min(FFN_N, N_SLABS - first)
                with sp.Fori(0, n // 12) as i:
                    for j in range(12):
                        load_slab(sp, first + j, i, 12)
                for j in range(n // 12 * 12, n):
                    load_slab(sp, first + j)
                sp.wait_ge(S["conv"], ONE + FT * 4)
                sp.dma_start(A["conv_rows"][layer], cout[:, :]).then_inc(S["out"], 16)
                sp.dma_start(A["conv_past"][layer], past[:, :, 1, :]).then_inc(S["out"], 16)
                sp.wait_ge(S["out"], ONE + 32)

            @block.tensor
            def _(pe):
                def up(n, i=0):
                    m = (6 * n - 2) + s0 if n else s0
                    for t in range(2):
                        for kind in range(2):
                            s = m + 2 * t + kind
                            per = 12 if n else 0
                            pe.wait_ge(lo_done, count(i, per, s + 1))
                            for ch in range(NCH):
                                before = 6 * n + 3 * t + ch - 2
                                done = S["a_in"] if kind == 0 else S["gate"]
                                if before > 0:
                                    pe.wait_ge(done, count(i, per, before))
                                if t == 0 and kind == 0 and n >= 1 and ch < 2:
                                    pe.wait_ge(S["yadd"], count(i, 2 * DOWN_J, DOWN_J * (n - 1)))
                                up_job(pe, bank[3 * kind + ch][:, 0:CH], s, ch).then_inc(jobs, 1)

                def down(n, i=0, loop=True):
                    s = s0 + 8 + 6 * n if n < NBLK - 1 else s0 + FFN_N - 2
                    per = 12 if loop else 0
                    pe.wait_ge(lo_done, count(i, per, s + 2))
                    pe.wait_ge(S["h_lo"], count(i, 4 if loop else 0, 2 * n + 2))
                    for q in range(DOWN_J):
                        ft, ch = divmod(q, NCH)
                        if q < 2:
                            if n < NBLK - 1:
                                if n >= 1 or loop:
                                    if n >= 1:
                                        pe.wait_ge(S["yadd"], count(i, 2 * DOWN_J if loop else 0, DOWN_J * n - 3 + q))
                                    else:
                                        pe.wait_ge(S["yadd"], count(i, 2 * DOWN_J, 0))
                            else:
                                pe.wait_ge(S["yadd"], ONE + DOWN_J * n - 3 + q)
                        elif q < 4:
                            if n < NBLK - 1:
                                pe.wait_ge(S["a_in"], count(i, 12 if loop else 0, 6 * (n + 1) + 3 + q - 1))
                            else:
                                pe.wait_ge(S["yadd"], ONE + DOWN_J * n - 3 + q)
                        else:
                            pe.wait_ge(S["yadd"], count(i, 2 * DOWN_J if loop else 0, DOWN_J * n + q - 3))
                        b = (6, 7, 0, 1)[q % 4]
                        down_job(pe, bank[b][:, 0:CH], s, ft, ch, hh[:, n % 2, :, :], hl[:, n % 2, :, :]).then_inc(jobs, 1)

                pe.wait_ge(S["in_"], ONE + 32)
                up(0)
                with pe.Fori(0, LOOPS) as i:
                    for n in range(2):
                        up(n + 1, i)
                        down(n, i)
                for i in range(LOOPS, (NBLK - 1) // 2):
                    for n in range(2):
                        up(n + 1, i)
                        down(n, i)
                down(NBLK - 1, loop=False)

            def ju(n):
                return j0 + (UP_J + (n - 1) * IT if n else 0)

            def jd(n):
                return j0 + UP_J + n * IT + (UP_J if n < NBLK - 1 else 0)

            @block.scalar
            def _(act):
                def up(n, i=0):
                    per = 1 if n else 0
                    s = s0 + (6 * n - 2 if n else 0)
                    for t in range(2):
                        for ch in range(NCH):
                            act.wait_ge(jobs, count(i, 2 * IT * per, ju(n) + 6 * t + ch + 1))
                            if ch == 0 and (n or t):
                                act.wait_ge(S["conv"], count(i, 16 * per, 4 * (2 * n + t)))
                            act.activation(ab[:, 2 + ch * CH:2 + (ch + 1) * CH], bank[ch][:, 0:CH],
                                           ACT.Copy).then_inc(S["a_in"], 1)
                        split_hi(act, s + 2 * t + AHEAD, i, 12 * per)
                        act.wait_ge(S["conv"], count(i, 16 * per, 4 * (2 * n + t) + 4))
                        act.activation(cv[:, :], cv[:, :], ACT.Silu).then_inc(S["silu"], 1)
                        split_hi(act, s + 2 * t + 1 + AHEAD, i, 12 * per)
                        act.wait_ge(S["gate"], count(i, 12 * per, 3 * (2 * n + t) + 3))
                        if n >= 2:
                            act.wait_ge(jobs, count(i, 2 * IT * per, jd(n - 2) + DOWN_J))
                        act.activation(hh[:, n % 2, t, :], hf[:, :], ACT.Copy).then_inc(S["h_hi"], 1)

                def down(n, i=0, loop=True):
                    s = s0 + 8 + 6 * n if n < NBLK - 1 else s0 + FFN_N - 2
                    per = 12 if loop else 0
                    for j in range(2):
                        split_hi(act, s + j + AHEAD, i, per)

                act.wait_ge(S["in_"], ONE + 32)
                act.wait_ge(S["border"], ONE + 1)
                up(0)
                with act.Fori(0, LOOPS) as i:
                    for n in range(2):
                        up(n + 1, i)
                        down(n, i)
                for i in range(LOOPS, (NBLK - 1) // 2):
                    for n in range(2):
                        up(n + 1, i)
                        down(n, i)
                down(NBLK - 1, loop=False)

            @block.vector
            def _(dve):
                def up(n, i=0):
                    per = 1 if n else 0
                    s = s0 + (6 * n - 2 if n else 0)
                    for t in range(2):
                        tile = 2 * n + t
                        at = plus(i, 4 * per, tile)

                        def tap(q):
                            return taps[:, 4 * tile + q:4 * tile + q + 1] if not per else taps[:, bass.ds(at * 4 + q, 1)]

                        def before(q):
                            if not per:
                                return past[:, tile, q, :]
                            return past[:, bass.ds(at, 1), q, :].rearrange("p a b -> p (a b)")
                        last = plus(i, 12 * per, 3 * (2 * n + t) + 3)
                        dve.wait_ge(S["a_in"], ONE + last)
                        if n or t:
                            dve.wait_ge(S["gate"], count(i, 12 * per, 3 * (2 * n + t)))
                        at4 = plus(i, 16 * per, 4 * (2 * n + t))
                        dve.tensor_scalar(cv[:, 0:SEQ], ab[:, 0:SEQ], tap(0), tap(3), ALU.mult, ALU.add)
                        dve.tensor_scalar(cv[:, SEQ:TOK], before(0), tap(0), tap(3), ALU.mult, ALU.add).then_inc(S["conv"], 1)
                        dve.wait_ge(S["conv"], ONE + at4 + 1)
                        dve.scalar_tensor_tensor(cv[:, 0:SEQ], ab[:, 1:SEQ + 1], tap(1), cv[:, 0:SEQ], ALU.mult, ALU.add)
                        dve.scalar_tensor_tensor(cv[:, SEQ:TOK], before(1), tap(1), cv[:, SEQ:TOK], ALU.mult,
                                                 ALU.add).then_inc(S["conv"], 1)
                        dve.wait_ge(S["conv"], ONE + at4 + 2)
                        dve.scalar_tensor_tensor(cv[:, :], ab[:, 2:TOK + 2], tap(2), cv[:, :], ALU.mult, ALU.add).then_inc(S["conv"], 1)
                        keep = cout[:, 10 * tile:10 * tile + 10] if not per else cout[:, bass.ds(at * 10, 10)]
                        dve.tensor_copy(keep, ab[:, SEQ:TOK + 2]).then_inc(S["conv"], 1)
                        split_lo(dve, s + 2 * t + AHEAD, i, 12 * per)
                        dve.wait_ge(S["silu"], count(i, 4 * per, 2 * n + t + 1))
                        for ch in range(NCH):
                            dve.wait_ge(jobs, count(i, 2 * IT * per, ju(n) + 6 * t + 3 + ch + 1))
                            if ch == 0 and (n or t):
                                dve.wait_ge(S["h_lo"], count(i, 4 * per, 2 * n + t))
                            dve.tensor_tensor(hf[:, columns(ch)], cv[:, columns(ch)], bank[3 + ch][:, 0:CH],
                                              ALU.mult).then_inc(S["gate"], 1)
                        split_lo(dve, s + 2 * t + 1 + AHEAD, i, 12 * per)

                def down(n, i=0, loop=True):
                    s = s0 + 8 + 6 * n if n < NBLK - 1 else s0 + FFN_N - 2
                    per = 12 if loop else 0
                    for q in range(DOWN_J):
                        ft, ch = divmod(q, NCH)
                        b = (6, 7, 0, 1)[q % 4]
                        dve.wait_ge(jobs, count(i, 2 * IT if loop else 0, jd(n) + q + 1))
                        dve.tensor_tensor(y[:, ft, columns(ch)], bank[b][:, 0:CH], y[:, ft, columns(ch)],
                                          ALU.add).then_inc(S["yadd"], 1)
                    for j in range(2):
                        split_lo(dve, s + j + AHEAD, i, per)

                dve.memset(ab[:, 0:2], 0.0).then_inc(S["border"], 1)
                dve.wait_ge(S["border"], ONE + 1)
                dve.wait_ge(S["in_"], ONE + 32)
                up(0)
                with dve.Fori(0, LOOPS) as i:
                    for n in range(2):
                        up(n + 1, i)
                        down(n, i)
                for i in range(LOOPS, (NBLK - 1) // 2):
                    for n in range(2):
                        up(n + 1, i)
                        down(n, i)
                down(NBLK - 1, loop=False)

            @block.gpsimd
            def _(pool):
                def up(n, i=0):
                    per = 1 if n else 0
                    for t in range(2):
                        pool.wait_ge(S["h_hi"], count(i, 4 * per, 2 * n + t + 1))
                        pool.tensor_tensor(hl[:, n % 2, t, :], hf[:, :], hh[:, n % 2, t, :].bitcast(F32),
                                           ALU.subtract).then_inc(S["h_lo"], 1)

                up(0)
                with pool.Fori(0, LOOPS) as i:
                    for n in range(2):
                        up(n + 1, i)
                for i in range(LOOPS, (NBLK - 1) // 2):
                    for n in range(2):
                        up(n + 1, i)


def retention_in(nc, A, env):
    ctx, sem, bank, plus, count = env["ctx"], env["sem"], env["bank"], env["plus"], env["count"]
    jobs, lo_done = env["jobs"], env["lo_done"]
    load_slab, split_hi, split_lo = env["load_slab"], env["split_hi"], env["split_lo"]
    columns, up_job = env["columns"], env["up_job"]
    S = {n: sem("p_" + n) for n in SEMS["p_"]}
    NT = 12
    TJ = NT * NCH
    with ExitStack() as c:
        def sb(name, shape, dt=F32):
            return c.enter_context(nc.sbuf_tensor("p_" + name, shape, dt))
        cosR = sb("cosR", [P, TOK])
        sinR = sb("sinR", [P, TOK])
        prod = sb("prod", [P, 4, TOK])
        rot = sb("rot", [P, 2, TOK])
        plain = sb("plain", [P, 2, TOK])

        with nc.Block() as block:
            @block.sync
            def _(sp):
                sp.dma_start(cosR[:, :], A["cosR"]).then_inc(S["in_"], 16)
                sp.dma_start(sinR[:, :], A["sinR"]).then_inc(S["in_"], 16)
                with sp.Fori(0, RH) as h:
                    for j in range(NT):
                        load_slab(sp, S_RIN + AHEAD + j, h, NT)

            @block.tensor
            def _(pe):
                with pe.Fori(0, RH) as h:
                    for j in range(NT):
                        pe.wait_ge(lo_done, count(h, NT, S_RIN + j + 1))
                        for ch in range(NCH):
                            b = 3 * (j % 2) + ch
                            if j < 2:
                                pe.wait_ge(S["plain"], count(h, 24, 0))
                            elif j < 4:
                                pe.wait_ge(S["prod"], count(h, 24, 4 * (ch + 1)))
                            elif j < 6:
                                pe.wait_ge(S["prod"], count(h, 24, 12 + 4 * (ch + 1)))
                            else:
                                pe.wait_ge(S["plain"], count(h, 24, 3 * (j - 6) + ch + 1))
                            up_job(pe, bank[b][:, 0:CH], S_RIN + j, ch).then_inc(jobs, 1)

            @block.scalar
            def _(act):
                with act.Fori(0, RH) as h:
                    for j in range(NT):
                        if j >= 4:
                            for ch in range(NCH):
                                act.wait_ge(jobs, count(h, TJ, J_RIN + 3 * j + ch + 1))
                                if ch == 0:
                                    n = j - 4
                                    act.wait_ge(S[f"out_p{n % 2}"], count(h, 64, 16 * (n // 2)))
                                act.activation(plain[:, j % 2, columns(ch)], bank[3 * (j % 2) + ch][:, 0:CH],
                                               ACT.Copy if j < 8 else ACT.Silu).then_inc(S["plain"], 1)
                            act.wait_ge(S["plain"], count(h, 24, 3 * (j - 4) + 3))
                            act.dma_start(A["scr"][bass.ds(h * NT + j, 1)].rearrange("a p n -> p (a n)"),
                                          plain[:, j % 2, :]).then_inc(S[f"out_p{j % 2}"], 16)
                        elif j % 2:
                            act.wait_ge(S["rot"], count(h, 4, j + 1))
                            for e in range(2):
                                act.dma_start(A["scr"][bass.ds(h * NT + j - 1 + e, 1)].rearrange("a p n -> p (a n)"),
                                              rot[:, e, :]).then_inc(S["out_r"], 16)
                        split_hi(act, S_RIN + j + AHEAD, h, NT)
                act.wait_ge(S["out_p0"], ONE + 16 * 4 * RH)
                act.wait_ge(S["out_p1"], ONE + 16 * 4 * RH)
                act.wait_ge(S["out_r"], ONE + 16 * 4 * RH)

            @block.vector
            def _(dve):
                dve.wait_ge(S["in_"], ONE + 32)
                with dve.Fori(0, RH) as h:
                    for j in range(NT):
                        if j in (1, 3):
                            for ch in range(NCH):
                                dve.wait_ge(jobs, count(h, TJ, J_RIN + 3 * j + ch + 1))
                                if ch == 0:
                                    dve.wait_ge(S["rot"], count(h, 4, j - 1))
                                t = columns(ch)
                                e, o = bank[ch][:, 0:CH], bank[3 + ch][:, 0:CH]
                                dve.tensor_tensor(prod[:, 0, t], e, cosR[:, t], ALU.mult).then_inc(S["prod"], 1)
                                dve.tensor_tensor(prod[:, 1, t], o, sinR[:, t], ALU.mult).then_inc(S["prod"], 1)
                                dve.tensor_tensor(prod[:, 2, t], o, cosR[:, t], ALU.mult).then_inc(S["prod"], 1)
                                dve.tensor_tensor(prod[:, 3, t], e, sinR[:, t], ALU.mult).then_inc(S["prod"], 1)
                        split_lo(dve, S_RIN + j + AHEAD, h, NT)

            @block.gpsimd
            def _(pool):
                with pool.Fori(0, RH) as h:
                    for pair in range(2):
                        pool.wait_ge(S["prod"], count(h, 24, 12 * (pair + 1)))
                        pool.wait_ge(S["out_r"], count(h, 64, 32 * pair))
                        pool.tensor_tensor(rot[:, 0, :], prod[:, 0, :], prod[:, 1, :], ALU.subtract).then_inc(S["rot"], 1)
                        pool.tensor_tensor(rot[:, 1, :], prod[:, 2, :], prod[:, 3, :], ALU.add).then_inc(S["rot"], 1)


def retention_core(nc, A, env):
    ctx, sem, bank, plus, count = env["ctx"], env["sem"], env["bank"], env["plus"], env["count"]
    ident, accumulate = env["ident"], env["accumulate"]
    S = {n: sem("r_" + n) for n in SEMS["r_"]}
    NT = 12
    with ExitStack() as c:
        def sb(name, shape, dt=F32):
            return c.enter_context(nc.sbuf_tensor("r_" + name, shape, dt))
        dec = sb("dec", [P, W + 5])
        onehot = sb("onehot", [NS, NS, P])
        m8 = sb("m8", [P, NS, NS])
        cx = sb("cx", [P, 2, NT, W])
        qkh = sb("qkh", [P, 4, W], F32R)
        qkl = sb("qkl", [P, 4, W], F32R)
        kdh = sb("kdh", [P, RK], F32R)
        kdl = sb("kdl", [P, RK], F32R)
        vh = sb("vh", [P, RV], F32R)
        vl = sb("vl", [P, RV], F32R)
        gt = sb("gt", [P, RV])
        inn = sb("inn", [P, W])
        ih = sb("ih", [P, W], F32R)
        il = sb("il", [P, W], F32R)
        st6 = sb("st6", [P, 6])
        st = sb("st", [P, 8])
        ga = sb("ga", [P, RV])
        ob = sb("ob", [P, 4, W])
        state = sb("state", [P, 2, RV])
        sh = sb("sh", [P, 2, RV], F32R)
        sl = sb("sl", [P, 2, RV], F32R)
        xs = sb("xs", [P, NT, NS])
        xv = sb("xv", [NS, RV])
        xg = sb("xg", [NS, RV])
        qm = sb("qm", [P, 2, NS, NS])
        k16 = sb("k16", [P, 2, NS])
        s0 = sb("s0", [P, 2, 2, RV])
        xst6 = sb("xst6", [NS, 6])
        xst = sb("xst", [NS, 8])
        xga = sb("xga", [NS, RV])
        xo = sb("xo", [P, 4, NS])

        kT, vT, gT, uB, kvB, sB, oT, xB = bank[0], bank[1], bank[2], bank[3], bank[4], bank[5], bank[6], bank[7]

        with nc.Block() as block:
            @block.sync
            def _(sp):
                sp.dma_start(onehot[:, :, :], A["onehot"]).then_inc(S["in_"], 16)
                sp.dma_start(m8[:, :, :], A["m8"]).then_inc(S["in_"], 16)
                sp.wait_ge(S["in_"], ONE + 32)
                with sp.Fori(0, RH) as h:
                    sp.wait_ge(S["s_lo"], count(h, NB, 0))
                    sp.sem_inc(S["passed"], 1)
                    sp.wait_ge(S["x_small"], count(h, 4, 0))
                    sp.sem_inc(S["passed"], 1)
                    sp.dma_start(dec[:, :], A["dec"][bass.ds(h, 1)].rearrange("a p n -> p (a n)")).then_inc(S["head_in"], 16)
                    sp.wait_ge(S["x_o"], count(h, NS, 0))
                    sp.sem_inc(S["passed"], 1)
                    sp.wait_ge(S["x_mask"], count(h, 2, 0))
                    sp.sem_inc(S["passed"], 1)
                    sp.dma_start(xs[:, :, :], A["scr"][bass.ds(h * NT, NT)].rearrange("a p n -> p a n")[:, :, SEQ:TOK])\
                      .then_inc(S["x_in"], 16)
                    for n in range(NB):
                        sp.wait_ge(S["turned"], count(h, NB, max(n - 1, 0)))
                        sp.sem_inc(S["passed"], 1)
                        sp.wait_ge(S["q_lo"], count(h, NB, max(n - 1, 0)))
                        sp.sem_inc(S["passed"], 1)
                        sp.dma_start(cx[:, n % 2, :, :],
                                     A["scr"][bass.ds(h * NT, NT)].rearrange("a p n -> p a n")[:, :, n * W:(n + 1) * W])\
                          .then_inc(S[f"qkvg{n % 2}"], 16)
                        sp.wait_ge(S[f"st_out{n % 2}"], count(h, 8 * NS, 16 * (n // 2)))
                        sp.sem_inc(S["passed"], 1)
                        sp.wait_ge(S["outer"], count(h, 2 * NS, 2 * max(n - 1, 0)))
                        sp.sem_inc(S["passed"], 1)
                        sp.wait_ge(S["x_o"], count(h, NS, max(n - 1, 0)))
                        sp.sem_inc(S["passed"], 1)
                        sp.dma_start(s0[:, n % 2, :, :], A["state_in"][n, bass.ds(h, 1)].rearrange("a p e n -> p (a e) n"))\
                          .then_inc(S[f"st_in{n % 2}"], 16)

            @block.tensor
            def _(pe):
                pe.wait_ge(S["in_"], ONE + 32)
                with pe.Fori(0, RH) as h:
                    def turn(n):
                        pe.wait_ge(S[f"qkvg{n % 2}"], count(h, 8 * NB, 16 * (n // 2) + 16))
                        pe.wait_ge(S["k_lo"], count(h, NB, n))
                        pe.wait_ge(S["v_lo"], count(h, NB, n))
                        pe.wait_ge(S["gate"], count(h, NB, n))
                        for j in range(2):
                            pe.transpose(kT[:, j * W:(j + 1) * W], cx[:, n % 2, 2 + j, :], ident[:, :])
                        for j in range(4):
                            pe.transpose(vT[:, j * W:(j + 1) * W], cx[:, n % 2, 4 + j, :], ident[:, :])
                        for j in range(4):
                            mm = pe.transpose(gT[:, j * W:(j + 1) * W], cx[:, n % 2, 8 + j, :], ident[:, :])
                        mm.then_inc(S["turned"], 1)

                    def inner(n):
                        pe.wait_ge(S["q_lo"], count(h, NB, n + 1))
                        pe.wait_ge(S["gated"], count(h, NB, n))
                        accumulate(pe, uB[:, 0:W],
                                   [(qkh[:, 2 + j, :], qkl[:, 2 + j, :], qkh[:, j, :], qkl[:, j, :]) for j in range(2)])\
                            .then_inc(S["inner"], 1)

                    def output(n):
                        pe.wait_ge(S["inner_lo"], count(h, NB, n + 1))
                        pe.wait_ge(S["v_lo"], count(h, NB, n + 1))
                        pe.wait_ge(S["s_lo"], count(h, NB, n))
                        pe.wait_ge(S["gated"], count(h, NB, n))
                        terms = [(ih[:, :], il[:, :], vh[:, :], vl[:, :])]
                        if n:
                            terms += [(qkh[:, j, :], qkl[:, j, :], sh[:, j, :], sl[:, j, :]) for j in range(2)]
                        accumulate(pe, uB[:, :], terms).then_inc(S["out_"], 1)

                    def update(n):
                        pe.wait_ge(S["k_lo"], count(h, NB, n + 1))
                        for j in range(2):
                            pe.wait_ge(S["state"], count(h, 2 * NB, 2 * n + j))
                            kk = slice(j * W, (j + 1) * W)
                            accumulate(pe, kvB[:, :], [(kdh[:, kk], kdl[:, kk], vh[:, :], vl[:, :])]).then_inc(S["kv"], 1)

                    def back(n):
                        pe.wait_ge(S["scaled"], count(h, NB, n + 1))
                        pe.wait_ge(S["back_c"], count(h, NB, n))
                        if n == 0:
                            pe.wait_ge(S["x_backc"], ONE + h)
                        for j in range(4):
                            mm = pe.transpose(oT[:, j * W:(j + 1) * W], ga[:, j * W:(j + 1) * W], ident[:, :])
                        mm.then_inc(S["back"], 1)

                    def sample_rows():
                        pe.wait_ge(S["x_in"], ONE + 16 * h + 16)
                        pe.wait_ge(S["x_rows"], ONE + 2 * h)
                        for j in range(4):
                            pe.transpose(sB[0:NS, j * W:(j + 1) * W], xs[:, 4 + j, :], ident[:, :])
                        for j in range(4):
                            mm = pe.transpose(xB[0:NS, j * W:(j + 1) * W], xs[:, 8 + j, :], ident[:, :])
                        mm.then_inc(S["x_turned"], 1)

                    def spread(b):
                        pe.wait_ge(S["x_rows"], ONE + 2 * h + 2)
                        pe.wait_ge(S["outer"], count(h, 2 * NS, 2 * b))
                        pe.matmul(sB[:, :], onehot[:, b, :], xv[:, :], start=True, stop=True).then_inc(S["spread"], 1)

                    def sample_out(b):
                        pe.wait_ge(S["x_mask"], ONE + 2 * h + 2)
                        pe.wait_ge(S["outer"], count(h, 2 * NS, 2 * b + 2))
                        for j in range(2):
                            mm = pe.matmul(xB[0:NS, :], qm[:, j, b, :], s0[:, b % 2, j, :], start=(b == 0 and j == 0),
                                           stop=(b == NS - 1 and j == 1))
                        mm.then_inc(S["x_o"], 1)

                    sample_rows()
                    for n in range(NB + 1):
                        if n < NB:
                            turn(n)
                            inner(n)
                            spread(n)
                            output(n)
                        if n:
                            back(n - 1)
                            sample_out(n - 1)
                        if n < NB:
                            update(n)
                    pe.wait_ge(S["x_gated"], ONE + h + 1)
                    pe.wait_ge(S["back_c"], count(h, NB, NB))
                    pe.sem_inc(S["passed"], 1)
                    for j in range(4):
                        mm = pe.transpose(oT[:, j * NS:(j + 1) * NS], xga[:, j * W:(j + 1) * W], ident[0:NS, 0:NS])
                    mm.then_inc(S["x_back"], 1)

            @block.scalar
            def _(act):
                act.wait_ge(S["in_"], ONE + 32)
                with act.Fori(0, RH) as h:
                    act.wait_ge(S["head_in"], ONE + 16 * h + 16)

                    def q_hi(n):
                        act.wait_ge(S[f"qkvg{n % 2}"], count(h, 8 * NB, 16 * (n // 2) + 16))
                        act.wait_ge(S["out_"], count(h, NB, n))
                        act.activation(qkh[:, :, :], cx[:, n % 2, 0:4, :], ACT.Copy).then_inc(S["q_hi"], 1)

                    def rows(n):
                        act.wait_ge(S["turned"], count(h, NB, n + 1))
                        act.wait_ge(S["kv"], count(h, 2 * NB, 2 * n))
                        act.activation(vh[:, :], vT[:, :], ACT.Copy).then_inc(S["v_hi"], 1)
                        act.activation(kdh[:, :], kT[:, 0:RK], ACT.Copy, scale=dec[:, W:W + 1]).then_inc(S["k_hi"], 1)
                        act.wait_ge(S["gated"], count(h, NB, n))
                        act.activation(gt[:, :], gT[:, :], ACT.Copy).then_inc(S["gate"], 1)

                    def inner_hi(n):
                        act.wait_ge(S["inner_d"], count(h, NB, n + 1))
                        act.activation(ih[:, :], inn[:, :], ACT.Copy).then_inc(S["inner_hi"], 1)

                    def root(n):
                        act.wait_ge(S["small"], count(h, 3 * NB, 3 * n + 1))
                        act.activation(st[:, 3:4], st[:, 2:3], ACT.Sqrt).then_inc(S["root"], 1)

                    def scale(n):
                        act.wait_ge(S["gated"], count(h, NB, n + 1))
                        act.wait_ge(S["small"], count(h, 3 * NB, 3 * n + 3))
                        act.activation(ga[:, :], ga[:, :], ACT.Copy, scale=st[:, 5:6]).then_inc(S["scaled"], 1)

                    def back(n):
                        act.wait_ge(S["back"], count(h, NB, n + 1))
                        act.wait_ge(S["o_out"], count(h, 16 * NB, 16 * n))
                        act.activation(ob[:, :, :], oT[:, :].rearrange("p (a n) -> p a n", a=4), ACT.Copy).then_inc(S["back_c"], 1)
                        act.wait_ge(S["back_c"], count(h, NB, n + 1))
                        act.dma_start(A["scr_o"][bass.ds(h * 4, 4)].rearrange("a p n -> p a n")[:, :, n * W:(n + 1) * W],
                                      ob[:, :, :]).then_inc(S["o_out"], 16)

                    def state_hi(n):
                        act.wait_ge(S["state"], count(h, 2 * NB, 2 * n + 2))
                        act.wait_ge(S["out_"], count(h, NB, n + 1))
                        act.activation(sh[:, :, :], state[:, :, :], ACT.Copy).then_inc(S["s_hi"], 1)

                    act.wait_ge(S["x_turned"], ONE + h + 1)
                    act.wait_ge(S["x_gated"], ONE + h)
                    act.activation(xv[:, :], sB[0:NS, :], ACT.Copy).then_inc(S["x_rows"], 1)
                    act.activation(xg[:, :], xB[0:NS, :], ACT.Copy).then_inc(S["x_rows"], 1)
                    for n in range(NB + 1):
                        if n < NB:
                            q_hi(n)
                            rows(n)
                            inner_hi(n)
                        if n:
                            back(n - 1)
                        if n < NB:
                            root(n)
                            scale(n)
                            state_hi(n)
                            act.wait_ge(S["outer"], count(h, 2 * NS, 2 * n + 2))
                            act.dma_start(A["state_s"][n, bass.ds(h, 1)].rearrange("a p e n -> p (a e) n"),
                                          s0[:, n % 2, :, :]).then_inc(S[f"st_out{n % 2}"], 16)
                    act.dma_start(A["state_p"][bass.ds(h, 1)].rearrange("a p e n -> p (a e) n"),
                                  state[:, :, :]).then_inc(S["s_out"], 16)
                    act.wait_ge(S["x_small"], ONE + 4 * h + 2)
                    act.activation(xst[:, 3:4], xst[:, 2:3], ACT.Sqrt).then_inc(S["x_root"], 1)
                    act.wait_ge(S["x_back"], ONE + h + 1)
                    act.wait_ge(S["x_out"], ONE + 16 * h)
                    act.activation(xo[:, :, :], oT[:, 0:4 * NS].rearrange("p (a n) -> p a n", a=4), ACT.Copy).then_inc(S["x_backc"], 1)
                    act.wait_ge(S["x_backc"], ONE + h + 1)
                    act.dma_start(A["scr_o"][bass.ds(h * 4, 4)].rearrange("a p n -> p a n")[:, :, SEQ:TOK],
                                  xo[:, :, :]).then_inc(S["x_out"], 16)
                act.wait_ge(S["o_out"], ONE + 16 * NB * RH)
                act.wait_ge(S["x_out"], ONE + 16 * RH)
                act.wait_ge(S["s_out"], ONE + 16 * RH)
                act.wait_ge(S["st_out0"], ONE + 8 * NS * RH)
                act.wait_ge(S["st_out1"], ONE + 8 * NS * RH)

            @block.vector
            def _(dve):
                dve.wait_ge(S["in_"], ONE + 32)
                with dve.Fori(0, RH) as h:
                    dve.wait_ge(S["head_in"], ONE + 16 * h + 16)

                    def rows(n):
                        dve.wait_ge(S["v_hi"], count(h, NB, n + 1))
                        dve.tensor_tensor(vl[:, :], vT[:, :], vh[:, :].bitcast(F32), ALU.subtract).then_inc(S["v_lo"], 1)
                        dve.wait_ge(S["k_hi"], count(h, NB, n + 1))
                        dve.scalar_tensor_tensor(kdl[:, :], kT[:, 0:RK], dec[:, W:W + 1], kdh[:, :].bitcast(F32),
                                                 ALU.mult, ALU.subtract).then_inc(S["k_lo"], 1)

                    def decay(n):
                        dve.wait_ge(S["inner"], count(h, NB, n + 1))
                        dve.wait_ge(S["inner_lo"], count(h, NB, n))
                        dve.tensor_tensor(inn[:, :], uB[:, 0:W], dec[:, 0:W], ALU.mult).then_inc(S["inner_d"], 1)
                        dve.wait_ge(S["inner_hi"], count(h, NB, n + 1))
                        dve.tensor_tensor(il[:, :], inn[:, :], ih[:, :].bitcast(F32), ALU.subtract).then_inc(S["inner_lo"], 1)

                    def norm(n):
                        dve.wait_ge(S["out_"], count(h, NB, n + 1))
                        dve.bn_stats(st6[:, :], uB[:, :]).then_inc(S["stats"], 1)
                        dve.wait_ge(S["stats"], count(h, 2 * NB, 2 * n + 1))
                        dve.wait_ge(S["scaled"], count(h, NB, n))
                        dve.sem_inc(S["passed"], 1)
                        dve.bn_aggr(st[:, 0:2], st6[:, :]).then_inc(S["stats"], 1)
                        dve.wait_ge(S["stats"], count(h, 2 * NB, 2 * n + 2))
                        dve.tensor_scalar(st[:, 2:3], st[:, 1:2], dec[:, W + 1:W + 2], EPS, ALU.mult, ALU.add).then_inc(S["small"], 1)
                        dve.wait_ge(S["gate"], count(h, NB, n + 1))
                        dve.wait_ge(S["back"], count(h, NB, n))
                        dve.scalar_tensor_tensor(ga[:, :], uB[:, :], st[:, 0:1], gt[:, :], ALU.subtract, ALU.mult)\
                           .then_inc(S["gated"], 1)
                        dve.wait_ge(S["root"], count(h, NB, n + 1))
                        dve.reciprocal(st[:, 4:5], st[:, 3:4]).then_inc(S["small"], 1)
                        dve.wait_ge(S["small"], count(h, 3 * NB, 3 * n + 2))
                        dve.tensor_scalar(st[:, 5:6], st[:, 4:5], dec[:, W + 2:W + 3], None, ALU.mult).then_inc(S["small"], 1)

                    def update(n):
                        for j in range(2):
                            dve.wait_ge(S["kv"], count(h, 2 * NB, 2 * n + j + 1))
                            if n:
                                if j == 0:
                                    dve.wait_ge(S["s_lo"], count(h, NB, n))
                                dve.scalar_tensor_tensor(state[:, j, :], state[:, j, :], dec[:, W + 3:W + 4], kvB[:, :],
                                                         ALU.mult, ALU.add).then_inc(S["state"], 1)
                            else:
                                if j == 0:
                                    dve.wait_ge(S["s_lo"], count(h, NB, 0))
                                    dve.wait_ge(S["s_out"], ONE + 16 * h)
                                dve.tensor_copy(state[:, j, :], kvB[:, :]).then_inc(S["state"], 1)

                    def outer(b):
                        dve.wait_ge(S["spread"], count(h, NS, b + 1))
                        dve.wait_ge(S["decay"], count(h, NS, b + 1))
                        for j in range(2):
                            dve.scalar_tensor_tensor(s0[:, b % 2, j, :], sB[:, :], k16[:, j, b:b + 1], s0[:, b % 2, j, :],
                                                     ALU.mult, ALU.add).then_inc(S["outer"], 1)

                    dve.wait_ge(S["x_in"], ONE + 16 * h + 16)
                    dve.wait_ge(S["x_o"], count(h, NS, 0))
                    for j in range(2):
                        a = dve.tensor_tensor(qm[:, j, :, :], m8[:, :, :], xs[:, j:j + 1, :].to_broadcast([P, NS, NS]), ALU.mult)
                    a.then_inc(S["x_mask"], 1)
                    dve.tensor_scalar(k16[:, :, :], xs[:, 2:4, :], RK ** -0.5, None, ALU.mult).then_inc(S["x_mask"], 1)
                    dve.wait_ge(S["x_mask"], ONE + 2 * h + 2)
                    for n in range(NB):
                        rows(n)
                        decay(n)
                        outer(n)
                        norm(n)
                        update(n)
                    dve.wait_ge(S["x_o"], count(h, NS, NS))
                    dve.bn_stats(xst6[:, :], xB[0:NS, :]).then_inc(S["x_stats"], 1)
                    dve.wait_ge(S["x_stats"], ONE + 2 * h + 1)
                    dve.sem_inc(S["passed"], 1)
                    dve.bn_aggr(xst[:, 0:2], xst6[:, :]).then_inc(S["x_stats"], 1)
                    dve.wait_ge(S["x_stats"], ONE + 2 * h + 2)
                    dve.tensor_scalar(xst[:, 6:7], xst[:, 0:1], -1.0, None, ALU.mult).then_inc(S["x_small"], 1)
                    dve.tensor_scalar(xst[:, 2:3], xst[:, 1:2], EPS, None, ALU.add).then_inc(S["x_small"], 1)
                    dve.wait_ge(S["x_root"], ONE + h + 1)
                    dve.reciprocal(xst[:, 4:5], xst[:, 3:4]).then_inc(S["x_small"], 1)
                    dve.wait_ge(S["x_back"], ONE + h)
                    dve.wait_ge(S["x_small"], ONE + 4 * h + 3)
                    dve.tensor_scalar(xga[:, :], xB[0:NS, :], xst[:, 0:1], xst[:, 4:5], ALU.subtract, ALU.mult).then_inc(S["x_small"], 1)
                    dve.wait_ge(S["x_small"], ONE + 4 * h + 4)
                    dve.tensor_tensor(xga[:, :], xga[:, :], xg[:, :], ALU.mult).then_inc(S["x_gated"], 1)

            @block.gpsimd
            def _(pool):
                pool.wait_ge(S["in_"], ONE + 32)
                with pool.Fori(0, RH) as h:
                    pool.wait_ge(S["head_in"], ONE + 16 * h + 16)
                    for n in range(NB):
                        pool.wait_ge(S["q_hi"], count(h, NB, n + 1))
                        pool.tensor_tensor(qkl[:, :, :], cx[:, n % 2, 0:4, :], qkh[:, :, :].bitcast(F32),
                                           ALU.subtract).then_inc(S["q_lo"], 1)
                        pool.wait_ge(S[f"st_in{n % 2}"], count(h, 8 * NS, 16 * (n // 2) + 16))
                        pool.sem_inc(S["passed"], 1)
                        pool.tensor_scalar(s0[:, n % 2, :, :], s0[:, n % 2, :, :], dec[:, W + 4:W + 5], None,
                                           ALU.mult).then_inc(S["decay"], 1)
                        pool.wait_ge(S["s_hi"], count(h, NB, n + 1))
                        pool.tensor_tensor(sl[:, :, :], state[:, :, :], sh[:, :, :].bitcast(F32), ALU.subtract).then_inc(S["s_lo"], 1)


def retention_out(nc, A, env):
    ctx, sem, bank = env["ctx"], env["sem"], env["bank"]
    y, jobs, lo_done = env["y"], env["jobs"], env["lo_done"]
    load_slab, split_hi, split_lo = env["load_slab"], env["split_hi"], env["split_lo"]
    columns, down_job = env["columns"], env["down_job"]
    S = {n: sem("o_" + n) for n in SEMS["o_"]}
    NO = 8
    with ExitStack() as c:
        def sb(name, shape, dt=F32):
            return c.enter_context(nc.sbuf_tensor("o_" + name, shape, dt))
        of = sb("of", [P, 2, TOK])
        oh = sb("oh", [P, 2, 2, TOK], F32R)
        ol = sb("ol", [P, 2, 2, TOK], F32R)
        with nc.Block() as block:
            @block.sync
            def _(sp):
                for n in range(NO):
                    if n:
                        sp.wait_ge(S["lo"], ONE + n)
                    sp.dma_start(of[:, :, :], A["scr_o"][2 * n:2 * n + 2].rearrange("a p n -> p a n")).then_inc(S["in_"], 16)
                    for j in range(2):
                        load_slab(sp, S_RO + AHEAD + 2 * n + j)

            @block.tensor
            def _(pe):
                for n in range(NO):
                    pe.wait_ge(lo_done, ONE + S_RO + 2 * n + 2)
                    pe.wait_ge(S["lo"], ONE + n + 1)
                    for q in range(DOWN_J):
                        ft, ch = divmod(q, NCH)
                        if n * DOWN_J + q >= 8:
                            pe.wait_ge(S["yadd"], ONE + n * DOWN_J + q - 7)
                        down_job(pe, bank[q % 8][:, 0:CH], S_RO + 2 * n, ft, ch, oh[:, n % 2, :, :], ol[:, n % 2, :, :])\
                            .then_inc(jobs, 1)

            @block.scalar
            def _(act):
                for n in range(NO + 1):
                    if n < NO:
                        act.wait_ge(S["in_"], ONE + 16 * n + 16)
                        if n >= 2:
                            act.wait_ge(jobs, ONE + J_RO + DOWN_J * (n - 1))
                        act.activation(oh[:, n % 2, :, :], of[:, :, :], ACT.Copy).then_inc(S["hi"], 1)
                    if n:
                        for j in range(2):
                            split_hi(act, S_RO + AHEAD + 2 * (n - 1) + j)

            @block.vector
            def _(dve):
                for n in range(NO + 1):
                    if n < NO:
                        dve.wait_ge(S["hi"], ONE + n + 1)
                        dve.tensor_tensor(ol[:, n % 2, :, :], of[:, :, :], oh[:, n % 2, :, :].bitcast(F32),
                                          ALU.subtract).then_inc(S["lo"], 1)
                    if n:
                        for q in range(DOWN_J):
                            ft, ch = divmod(q, NCH)
                            dve.wait_ge(jobs, ONE + J_RO + DOWN_J * (n - 1) + q + 1)
                            dve.tensor_tensor(y[:, ft, columns(ch)], bank[q % 8][:, 0:CH], y[:, ft, columns(ch)],
                                              ALU.add).then_inc(S["yadd"], 1)
                        for j in range(2):
                            split_lo(dve, S_RO + AHEAD + 2 * (n - 1) + j)


def tables():
    f = np.float32
    pos = np.concatenate([np.arange(SEQ), np.full(NS, SEQ)]).astype(f)
    half = HD // 2
    inv = (f(10000.0) ** (-np.arange(half, dtype=f) / f(half))).astype(f)
    ang = (np.concatenate([np.arange(SEQ), np.full(P, SEQ)]).astype(f)[:, None] * inv[None, :]).astype(f)

    def by_block(t):
        return np.ascontiguousarray(t.astype(f).reshape(NB + 1, P, half).transpose(1, 0, 2))
    ca = np.cos(ang.astype(np.float64))
    sa = np.sin(ang.astype(np.float64))
    angle = (f(1.0) / (f(10000.0) ** np.linspace(0.0, 1.0, RK // 2, dtype=f))).astype(f)
    angr = (angle[:, None] * pos[None, :]).astype(f).astype(np.float64)
    i = np.arange(W)
    mask = np.zeros((P, 2 * W), f)
    mask[:, :W][i[None, :] < i[:, None]] = NEG
    mask[:, W:][i[None, :] > i[:, None]] = NEG
    dec = np.zeros((RH, P, W + 5), f)
    for h in range(RH):
        lg = np.log1p(-(2.0 ** (-5.0 - h)))
        inner = np.exp(-lg * (i + 1.0))[:, None] * (i[:, None] <= i[None, :]) * RK ** -0.5
        dec[h, :, 0:W] = inner
        dec[h, :, W] = np.exp(lg * (W - 1.0 - i)) * RK ** -0.5
        dec[h, :, W + 1] = np.exp(2 * lg * (i + 1.0))
        dec[h, :, W + 2] = np.exp(lg * (i + 1.0))
        dec[h, :, W + 3] = np.exp(lg * W)
        dec[h, :, W + 4] = np.exp(lg)
    eye = np.eye(NS, dtype=f)
    return {
        "ident": np.eye(P, dtype=f), "ones": np.full((P, P), 1.0 / D, f),
        "cosT": by_block(ca), "sinT": by_block(sa), "mask": mask,
        "cosR": np.cos(angr).astype(f), "sinR": np.sin(angr).astype(f), "dec": dec,
        "same": np.repeat(eye, GH, axis=0),
        "onehot": np.repeat(eye[:, :, None], P, axis=2),
        "m8": np.repeat(eye[None], P, axis=0),
    }


def kernel(**inputs):
    import concourse.bacc as bacc
    from concourse.bass_utils import run_bass_kernel_spmd

    a = {n: np.asarray(v) for n, v in inputs.items()}

    def up_slabs(w, starts):
        return [w[:, s:s + P].reshape(KT, P, P).transpose(1, 0, 2).reshape(P, SLAB) for s in starts]

    qkv, wo = a["attn_w_qkv"][0], a["attn_w_o"][0]
    rin, ro = a["ret_w_in"][0], a["ret_w_o"][0]
    slabs = []
    for g in range(NG):
        cols = np.concatenate([qkv[:, g * 256:(g + 1) * 256], qkv[:, D + g * HD:D + (g + 1) * HD],
                               qkv[:, D + 256 + g * HD:D + 256 + (g + 1) * HD]], axis=1)
        slabs += up_slabs(cols, (0, P, 2 * P))
        slabs += [wo[g * 256:g * 256 + P], wo[g * 256 + P:(g + 1) * 256]]

    def ffn(layer):
        wi, wo_ = a["ffn_w_in"][layer], a["ffn_w_out"][layer]
        out = []
        for n in range(NBLK + 1):
            if n < NBLK:
                out += up_slabs(wi, (2 * n * P, FF + 2 * n * P, (2 * n + 1) * P, FF + (2 * n + 1) * P))
            if n:
                out += [wo_[(2 * n - 2 + j) * P:(2 * n - 1 + j) * P] for j in range(2)]
        return out
    slabs += ffn(0)
    for h in range(RH):
        for part in range(2):
            w = rin[:, part * D + h * RK:part * D + (h + 1) * RK]
            slabs += up_slabs(w[:, 0::2], (0,)) + up_slabs(w[:, 1::2], (0,))
        for part in range(2):
            s = 2 * D + part * RH * RV + h * RV
            slabs += up_slabs(rin, range(s, s + RV, P))
    slabs += [ro[n * P:(n + 1) * P] for n in range(16)]
    slabs += ffn(1)

    def tiles(v, n):
        return np.moveaxis(v.reshape(v.shape[:-1] + (n, P)), -1, 0)

    x = np.concatenate([a["x_prompt"][0], a["x_sample"][:, 0]], axis=0)
    taps = np.concatenate([a["ffn_conv_w"], a["ffn_conv_b"][:, None]], axis=1)
    ins = {
        "w": np.stack(slabs),
        "x": x.T.reshape(KT, P, TOK).transpose(1, 0, 2),
        "kcache": a["cache_k_win"][0].transpose(2, 3, 0, 1),
        "vcache": a["cache_v_win"][0].transpose(2, 1, 0, 3),
        "kcache_rows": a["cache_k_win"][0],
        "vcache_rows": a["cache_v_win"][0],
        "sinkb": np.repeat(a["attn_sinks"], P, axis=0),
        "sinkc": np.tile(a["attn_sinks"][0].reshape(NG, GH).T, (NS, 1)),
        "state_in": a["state_ret"][0].reshape(NS, RH, P, 2, RV),
        "past": np.stack([a["state_conv"][n].transpose(2, 1, 0).reshape(FT, P, 2, NS).transpose(1, 0, 2, 3) for n in range(2)]),
        "taps": np.stack([tiles(taps[n], FT).transpose(0, 2, 1).reshape(P, FT * 4) for n in range(2)]),
        "ln_mix": np.stack([tiles(np.stack([a["ln_mix_g"][n], a["ln_mix_b"][n]]), KT) for n in range(2)]),
        "ln_ffn": np.stack([tiles(np.stack([a["ln_ffn_g"][n], a["ln_ffn_b"][n]]), KT) for n in range(2)]),
        **tables(),
    }
    ins = {n: np.ascontiguousarray(v) for n, v in ins.items()}
    outs = {
        "y": (P, KT, TOK), "kwin_p": (W, NG, HD), "vwin_p": (W, NG, HD), "kwin_s": (NS, W, NG, HD),
        "vwin_s": (NS, W, NG, HD), "state_p": (RH, P, 2, RV), "state_s": (NS, RH, P, 2, RV),
        "conv_rows": (2, P, FT * 10), "conv_past": (2, P, FT, NS),
    }
    nc = bacc.Bacc("TRN2", target_bir_lowering=False, num_devices=1, dynamic_dma_scratch_size=512)
    A = {n: nc.dram_tensor("in_" + n, v.shape, F32, kind="ExternalInput").ap() for n, v in ins.items()}
    A |= {n: nc.dram_tensor("out_" + n, s, F32, kind="ExternalOutput").ap() for n, s in outs.items()}
    A["scr"] = nc.dram_tensor("scratch_qkvg", (12 * RH, P, TOK), F32, kind="Internal").ap()
    A["scr_o"] = nc.dram_tensor("scratch_heads", (16, P, TOK), F32, kind="Internal").ap()
    build(nc, A)
    r = run_bass_kernel_spmd(nc, [{"in_" + n: v for n, v in ins.items()}], core_ids=[0]).results[0]
    r = {n: np.asarray(r["out_" + n]) for n in outs}

    yt = r["y"].transpose(1, 0, 2).reshape(D, TOK).T
    rows = r["conv_rows"].reshape(2, P, FT, 10).transpose(0, 3, 2, 1).reshape(2, 10, FF)
    past = r["conv_past"].transpose(0, 3, 2, 1).reshape(2, NS, FF)
    return (np.ascontiguousarray(yt[:SEQ])[None], np.ascontiguousarray(yt[SEQ:])[:, None],
            r["kwin_p"][None, None], r["vwin_p"][None, None],
            r["state_p"].reshape(1, 1, RH, RK, RV),
            np.ascontiguousarray(rows[:, None, 0:2]),
            r["kwin_s"][None], r["vwin_s"][None],
            r["state_s"].reshape(1, NS, RH, RK, RV),
            np.stack([past, rows[:, 2:]], axis=2))
```

```python
import numpy as np
import concourse.bass as bass
from concourse import mybir
from contextlib import ExitStack

F32 = mybir.dt.float32
F32R = mybir.dt.float32r
ALU = mybir.AluOpType
ACT = mybir.ActivationFunctionType
AXX = mybir.AxisListType.X

P = 128
D = 1024
SEQ = 1024
NS = 8
TOK = SEQ + NS
KT = D // P
NCH = 3
CH = TOK // NCH
HD = 64
NG = 4
GH = 4
W = 128
NB = SEQ // W
RH = 4
RK = 256
RV = 512
FF = 2816
FT = FF // P
NBLK = FT // 2
ALPHA = (2.0 * 2) ** 0.25
EPS = 1e-5
NEG = -1e30
LN_BIG = -3e38

SLAB = 1024
RING = 6
ATT_S = 5
ATT_N = NG * ATT_S
FFN_N = 6 * NBLK
S_ATT, S_FFN0 = 0, ATT_N
S_RIN = S_FFN0 + FFN_N
S_RO = S_RIN + 12 * RH
S_FFN1 = S_RO + 16
N_SLABS = S_FFN1 + FFN_N
AHEAD = 5


RAW = 3


def raw_slot(s):
    return s % ATT_S % RAW if s < ATT_N else (s - ATT_N) % RAW


def raw_use(s):
    return sum(raw_slot(n) == raw_slot(s) for n in range(s + 1))


def slot(s):
    return s % ATT_S if s < ATT_N else (s - ATT_N) % RING


UP_J, DOWN_J = 4 * NCH, KT * NCH
ATT_J = (NB + 1) + DOWN_J
FFN_J = NBLK * (UP_J + DOWN_J)
J_FFN0 = NG * ATT_J
J_RIN = J_FFN0 + FFN_J
J_RO = J_RIN + 12 * RH * NCH
J_FFN1 = J_RO + 8 * DOWN_J


def ended(s):
    if s < S_FFN0:
        g, j = divmod(s, ATT_S)
        return g * ATT_J + (NB + 1 if j < 3 else ATT_J)
    if s < S_RIN or s >= S_FFN1:
        j0, r = (J_FFN0, s - S_FFN0) if s < S_RIN else (J_FFN1, s - S_FFN1)
        if r < 4:
            return j0 + NCH * (r + 1)
        b, q = divmod(r - 4, 6)
        if b == NBLK - 1:
            return j0 + FFN_J
        return j0 + UP_J + b * (UP_J + DOWN_J) + (NCH * (q + 1) if q < 4 else UP_J + DOWN_J)
    if s < S_RO:
        return J_RIN + NCH * (s - S_RIN + 1)
    return J_RO + DOWN_J * ((s - S_RO) // 2 + 1)


ONE = 1
SEMS = {
    "": ("raw_in0 raw_in1 raw_in2 hi_done lo_done jobs x_in0 x_in1 x_in2 c_in x_hi x_lo x_y").split(),
    "a_": ("table_in cache_in rope_t v_hi v_fp v_free qk back t_hi t_lo score shifted small small2 expd "
             "inv probs pt pt_hi pt_lo heads heads_hi heads_lo yadd kv_out win_out s_sc s_scc "
             "s_tr s_mx s_ex s_p s_pt s_ptc s_o s_oh s_ol dchain passed").split(),
    "n_": "in_ mean centred squares var eps std inv scaled bias hi lo shift out".split(),
    "f0_": "in_ border a_in conv silu gate h_hi h_lo yadd out".split(),
    "f1_": "in_ border a_in conv silu gate h_hi h_lo yadd out".split(),
    "p_": "in_ prod rot plain out_r out_p0 out_p1".split(),
    "r_": ("in_ head_in qkvg0 qkvg1 turned q_hi q_lo k_hi k_lo v_hi v_lo gate inner inner_d inner_hi inner_lo out_ "
             "stats small root gated scaled back back_c o_out kv state s_hi s_lo s_out "
             "x_in x_turned x_rows x_mask st_in0 st_in1 decay spread outer x_o x_stats x_small x_root x_gated x_back x_backc "
             "x_out st_out0 st_out1 passed").split(),
    "o_": "in0 in1 hi lo yadd".split(),
}

LN_COUNTS = {"in_": 16, "bias": 1, "shift": NCH, "out": 0} | dict.fromkeys(
    "mean centred squares var eps std inv scaled hi lo".split(), NCH)


def build(nc, A):
    ctx = ExitStack()
    with ctx:
        def sb(name, shape, dt=F32, c=ctx):
            return c.enter_context(nc.sbuf_tensor(name, shape, dt))

        sems = {p + n: ctx.enter_context(nc.semaphore(p + n)) for p, names in SEMS.items() for n in names}

        def sem(name):
            return sems[name]

        raw = sb("raw", [P, RAW, SLAB])
        wh = sb("wh", [P, RING, SLAB], F32R)
        wl = sb("wl", [P, RING, SLAB], F32R)
        xh = sb("xh", [P, KT, TOK], F32R)
        xl = sb("xl", [P, KT, TOK], F32R)
        y = sb("y", [P, KT, TOK])
        ident = sb("ident", [P, P])
        ones = sb("ones", [P, P])
        bank = [ctx.enter_context(nc.psum_tensor(f"bank{n}", [P, 512], F32)) for n in range(8)]

        raw_in = [sem(f"raw_in{n}") for n in range(RAW)]
        hi_done = sem("hi_done")
        lo_done = sem("lo_done")
        jobs = sem("jobs")

        def plus(i, per, base):
            return base if per == 0 else i * per + base

        def count(i, per, base):
            return plus(i, per, ONE + base)

        def load_slab(sp, s, i=0, n=0):
            if s >= 2:
                sp.wait_ge(lo_done, count(i, n, s - 1))
            src = A["w"][s] if n == 0 else A["w"][bass.ds(i * n + s, 1)].rearrange("a p n -> p (a n)")
            sp.dma_start(raw[:, raw_slot(s), :], src).then_inc(raw_in[raw_slot(s)], 16)

        def split_hi(act, s, i=0, n=0):
            if s >= N_SLABS or (isinstance(i, int) and s + i * n >= N_SLABS):
                return
            act.wait_ge(raw_in[raw_slot(s)], count(i, 16 * (raw_use(s + n) - raw_use(s)), 16 * raw_use(s)))
            if s >= AHEAD:
                act.wait_ge(jobs, count(i, ended(s - AHEAD + n) - ended(s - AHEAD), ended(s - AHEAD)))
            act.activation(wh[:, slot(s), :], raw[:, raw_slot(s), :], ACT.Copy).then_inc(hi_done, 1)

        def split_lo(dve, s, i=0, n=0):
            if s >= N_SLABS or (isinstance(i, int) and s + i * n >= N_SLABS):
                return
            dve.wait_ge(hi_done, count(i, n, s + 1))
            dve.tensor_tensor(wl[:, slot(s), :], raw[:, raw_slot(s), :], wh[:, slot(s), :].bitcast(F32),
                              ALU.subtract).then_inc(lo_done, 1)

        def columns(c):
            return slice(c * CH, (c + 1) * CH)

        def accumulate(pe, out, terms):
            n = len(terms)
            for k, (ah, al, bh, bl) in enumerate(terms):
                pe.matmul(out, ah, bh, start=(k == 0), stop=False)
                pe.matmul(out, ah, bl, start=False, stop=False)
                mm = pe.matmul(out, al, bh, start=False, stop=(k == n - 1))
            return mm

        def up_job(pe, out, s, c):
            def tile(w, k):
                return w[:, slot(s), k * P:(k + 1) * P]
            return accumulate(pe, out, [(tile(wh, k), tile(wl, k), xh[:, k, columns(c)], xl[:, k, columns(c)])
                                        for k in range(KT)])

        def down_job(pe, out, s, ft, c, mh, ml):
            def tile(w, k):
                return w[:, slot(s + k), ft * P:(ft + 1) * P]
            return accumulate(pe, out, [(tile(wh, k), tile(wl, k), mh[:, k, columns(c)], ml[:, k, columns(c)])
                                        for k in range(2)])

        x_in = [sem(f"x_in{ch}") for ch in range(NCH)]
        c_in = sem("c_in")
        x_hi = sem("x_hi")
        x_lo = sem("x_lo")
        x_y = sem("x_y")
        with nc.Block() as block:
            def set_one(eng, n):
                for name in list(sems)[n::5]:
                    eng.sem_inc(sems[name], ONE)

            @block.sync
            def _(sp):
                set_one(sp, 0)

            @block.scalar
            def _(act):
                set_one(act, 1)

            @block.vector
            def _(dve):
                set_one(dve, 2)

            @block.tensor
            def _(pe):
                set_one(pe, 3)

            @block.gpsimd
            def _(pool):
                set_one(pool, 4)

        with nc.Block() as block:
            @block.sync
            def _(sp):
                for s in range(AHEAD):
                    load_slab(sp, s)

            @block.scalar
            def _(act):
                for ch in range(NCH):
                    act.dma_start(y[:, :, columns(ch)], A["x"][:, :, columns(ch)]).then_inc(x_in[ch], 16)
                act.dma_start(ident[:, :], A["ident"]).then_inc(c_in, 16)
                act.dma_start(ones[:, :], A["ones"]).then_inc(c_in, 16)
                for ch in range(NCH):
                    act.wait_ge(x_in[ch], ONE + 16)
                    act.activation(xh[:, :, columns(ch)], y[:, :, columns(ch)], ACT.Copy).then_inc(x_hi, 1)
                    split_hi(act, ch)
                for s in range(NCH, AHEAD):
                    split_hi(act, s)
                for ch in range(1, NCH):
                    act.wait_ge(x_lo, ONE + ch + 1)
                    act.activation(y[:, :, columns(ch)], y[:, :, columns(ch)], ACT.Copy, scale=ALPHA).then_inc(x_y, 1)
                act.wait_ge(c_in, ONE + 32)

            @block.vector
            def _(dve):
                for ch in range(NCH):
                    dve.wait_ge(x_hi, ONE + ch + 1)
                    dve.tensor_tensor(xl[:, :, columns(ch)], y[:, :, columns(ch)], xh[:, :, columns(ch)].bitcast(F32),
                                      ALU.subtract).then_inc(x_lo, 1)
                    split_lo(dve, ch)
                for s in range(NCH, AHEAD):
                    split_lo(dve, s)

            @block.gpsimd
            def _(pool):
                pool.wait_ge(x_lo, ONE + 1)
                pool.tensor_scalar(y[:, :, columns(0)], y[:, :, columns(0)], ALPHA, None, ALU.mult).then_inc(x_y, 1)

        S_ln = {n: sem("n_" + n) for n in LN_COUNTS}
        attention(nc, A, locals())
        layer_norm(nc, A, locals(), 0, "mix", True)
        conv_ffn(nc, A, locals(), 0)
        layer_norm(nc, A, locals(), 0, "ffn", True)
        retention_in(nc, A, locals())
        retention_core(nc, A, locals())
        retention_out(nc, A, locals())
        layer_norm(nc, A, locals(), 1, "mix", True)
        conv_ffn(nc, A, locals(), 1)
        layer_norm(nc, A, locals(), 1, "ffn", False)


def attention(nc, A, env):
    ctx, sem, bank, plus, count = env["ctx"], env["sem"], env["bank"], env["plus"], env["count"]
    xh, xl, y, wh, wl, ident = (env[n] for n in ("xh", "xl", "y", "wh", "wl", "ident"))
    jobs, lo_done = env["jobs"], env["lo_done"]
    load_slab, split_hi, split_lo = env["load_slab"], env["split_hi"], env["split_lo"]
    columns, accumulate, down_job = env["columns"], env["accumulate"], env["down_job"]
    S = {n: sem("a_" + n) for n in SEMS["a_"]}
    KR, VR = 3, 6

    with ExitStack() as c:
        def sb(name, shape, dt=F32):
            return c.enter_context(nc.sbuf_tensor("a_" + name, shape, dt))
        cosT = sb("cosT", [P, NB + 1, 32])
        sinT = sb("sinT", [P, NB + 1, 32])
        mask = sb("mask", [P, 2 * W])
        sinkb = sb("sinkb", [P, NG * GH])
        sinkc = sb("sinkc", [32, NG])
        same = sb("same", [32, NS])
        t1 = sb("t1", [P, 2, 320])
        t2 = sb("t2", [P, 2, 320])
        qk = sb("qk", [P, 2, 384])
        vh = sb("vh", [P, VR, 2, HD], F32R)
        vl = sb("vl", [P, VR, 2, HD], F32R)
        vf = sb("vf", [P, 2, HD])
        vs2 = sb("vs2", [NS, 2, HD])
        qh = sb("qh", [P, 256], F32R)
        ql = sb("ql", [P, 256], F32R)
        kh = sb("kh", [P, KR * W], F32R)
        kl = sb("kl", [P, KR * W], F32R)
        sm = sb("sm", [P, GH, 2 * W])
        prob = sb("prob", [P, GH, 2 * W])
        st = sb("st", [P, 8, GH])
        pth = sb("pth", [P, 2, GH * W], F32R)
        ptl = sb("ptl", [P, 2, GH * W], F32R)
        oh = sb("oh", [P, 2, TOK], F32R)
        ol = sb("ol", [P, 2, TOK], F32R)
        sq = sb("sq", [P, 3, NS])
        kc = sb("kc", [P, NS, W])
        vc = sb("vc", [P, NS, 2, HD])
        ss = sb("ss", [P, 32])
        row = sb("row", [1, 32])
        sp_ = sb("sp", [32, W + 1])
        sst = sb("sst", [32, 8])
        spt = sb("spt", [P, 32])
        dg = sb("dg", [32, 32])
        pn = sb("pn", [NS, 32])

        def down_bank(q):
            return bank[q % 2 if q < 2 * KT else (0, 1, 3, 4)[q % 4]][:, 0:CH]

        with nc.Block() as block:
            @block.sync
            def _(sp):
                for n, t in (("cosT", cosT), ("sinT", sinT), ("mask", mask), ("sinkb", sinkb), ("sinkc", sinkc), ("same", same)):
                    sp.dma_start(t[tuple([slice(None)] * len(t.shape))], A[n]).then_inc(S["table_in"], 16)
                with sp.Fori(0, NG) as g:
                    sp.wait_ge(S["s_o"], ONE + g)
                    kcg = A["kcache"][bass.ds(g, 1)].rearrange("a d b k -> d (a b) k")
                    sp.dma_start(kc[0:HD, :, :], kcg).then_inc(S["cache_in"], 16)
                    sp.dma_start(kc[HD:P, :, :], kcg).then_inc(S["cache_in"], 16)
                    vcg = A["vcache"][bass.ds(g, 1)].rearrange("a k b d -> k (a b) d")
                    sp.dma_start(vc[:, :, 0, :], vcg).then_inc(S["cache_in"], 16)
                    sp.dma_start(vc[:, :, 1, :], vcg).then_inc(S["cache_in"], 16)
                    for j in range(ATT_S):
                        load_slab(sp, AHEAD + j, g, ATT_S)
                sp.dma_start(A["kwin_s"][:, 0:W - 1, :, :], A["kcache_rows"][:, 1:W, :, :]).then_inc(S["win_out"], 16)
                sp.dma_start(A["vwin_s"][:, 0:W - 1, :, :], A["vcache_rows"][:, 1:W, :, :]).then_inc(S["win_out"], 16)
                sp.wait_ge(S["win_out"], ONE + 32)

            @block.tensor
            def _(pe):
                with pe.Fori(0, NG) as g:
                    def project(b):
                        m = P if b < NB else NS
                        if b == 0:
                            pe.wait_ge(lo_done, count(g, ATT_S, 3))
                            pe.wait_ge(S["yadd"], count(g, DOWN_J, 0))
                        if b >= 2:
                            pe.wait_ge(S["v_free"], count(g, NB, b - 1))
                        o = bank[b % 2][0:m, 0:384].rearrange("m (a n) -> m a n", a=3)
                        terms = []
                        for k in range(KT):
                            t = slice(b * W, b * W + m)
                            kk = slice(k * P, (k + 1) * P)
                            terms.append((xh[:, k, t], xl[:, k, t], wh[:, 0:3, kk], wl[:, 0:3, kk]))
                        accumulate(pe, o, terms).then_inc(jobs, 1)

                    def turn(b):
                        m = P if b < NB else NS
                        pe.wait_ge(S["qk"], count(g, 2 * (NB + 1), 2 * b + 2))
                        if b >= 1:
                            pe.wait_ge(S["t_lo"], count(g, 2 * NB + 1, 2 * b))
                        pe.sem_inc(S["passed"], 1)
                        for j in range(3):
                            t = pe.transpose(bank[2][:, j * P:j * P + m], qk[0:m, b % 2, j * P:(j + 1) * P],
                                             ident[0:m, 0:m])
                        t.then_inc(S["back"], 1)

                    def scores(b):
                        pe.wait_ge(S["t_lo"], count(g, 2 * NB + 1, 2 * b + 2))
                        if b >= 1:
                            pe.wait_ge(S["shifted"], count(g, GH * NB, GH * b))
                        kb = b % KR * W
                        pieces = [(kb, W, W)] if b == 0 else [(kb - W, 0, 2 * W)] if b % KR else [((KR - 1) * W, 0, W), (0, W, W)]
                        for h in range(GH):
                            r = slice(HD * (h % 2), HD * (h % 2) + HD)
                            q = slice(W * (h // 2), W * (h // 2) + W)
                            for k0, at, n in pieces:
                                o = bank[3 + h % 2][:, (h // 2) * 256 + at:(h // 2) * 256 + at + n]
                                mm = accumulate(pe, o, [(qh[r, q], ql[r, q], kh[r, k0:k0 + n], kl[r, k0:k0 + n])])
                        mm.then_inc(S["score"], 1)

                    def turn_probs(b):
                        pe.wait_ge(S["probs"], count(g, NB, b + 1))
                        if b >= 1:
                            pe.wait_ge(S["pt_lo"], count(g, NB, b))
                        for t in range(0 if b else 1, 2):
                            for h in range(GH):
                                mm = pe.transpose(bank[5 + t][:, h * W:(h + 1) * W], prob[:, h, t * W:(t + 1) * W],
                                                  ident[:, :])
                        mm.then_inc(S["pt"], 1)

                    def values(b):
                        pe.wait_ge(S["pt_lo"], count(g, NB, b + 1))
                        if b >= 1:
                            pe.wait_ge(S["heads_lo"], count(g, NB, b))
                        terms = []
                        for t in range(0 if b else 1, 2):
                            v = b - 1 + t
                            terms.append((vh[:, v % VR, :, :], vl[:, v % VR, :, :], pth[:, t, :], ptl[:, t, :]))
                        accumulate(pe, bank[7][:, :], terms).then_inc(S["heads"], 1)

                    def sample_scores():
                        pe.wait_ge(S["t_lo"], count(g, 2 * NB + 1, 2 * NB + 1))
                        pe.wait_ge(S["shifted"], count(g, GH * NB, GH * NB))
                        pe.wait_ge(S["cache_in"], count(g, 64, 64))
                        for b in range(NS):
                            for h in range(2):
                                r = slice(HD * h, HD * h + HD)
                                pe.matmul(bank[3 + h][:, b * 4 + h:b * 4 + 4:2], kc[r, b, :], sq[r, 0:2, b],
                                          start=True, stop=True)
                        for b in range(NS):
                            for h in range(2):
                                r = slice(HD * h, HD * h + HD)
                                mm = pe.matmul(bank[3 + h][0:1, 32 + b * 4 + h:32 + b * 4 + 4:2], sq[r, 2, b:b + 1],
                                               sq[r, 0:2, b], start=True, stop=True)
                        mm.then_inc(S["s_sc"], 1)

                    def sample_turn():
                        pe.wait_ge(S["s_scc"], ONE + 4 * g + 4)
                        pe.sem_inc(S["passed"], 1)
                        pe.transpose(bank[2][0:32, 0:W], ss[:, :], ident[:, :])
                        pe.matmul(bank[2][0:32, W:W + 1], row[:, :], ident[0:1, 0:1], start=True,
                                  stop=True).then_inc(S["s_tr"], 1)

                    def sample_turn_probs():
                        pe.wait_ge(S["table_in"], ONE + 16 * 6)
                        pe.wait_ge(S["dchain"], count(g, 4, 4))
                        pe.wait_ge(S["s_p"], ONE + g + 1)
                        pe.wait_ge(S["pt_lo"], count(g, NB, NB))
                        pe.sem_inc(S["passed"], 1)
                        pe.transpose(bank[5][:, 0:32], sp_[:, 0:W], ident[0:32, 0:32])
                        pe.matmul(bank[6][0:NS, 0:32], same[:, :], dg[:, :], start=True, stop=True).then_inc(S["s_pt"], 1)

                    def sample_values():
                        pe.wait_ge(S["s_ptc"], ONE + 2 * g + 2)
                        for b in range(NS):
                            o = bank[2][:, b * 4:b * 4 + 4]
                            pe.matmul(o, vc[:, b, :, :], spt[:, b * 4:b * 4 + 4], start=True, stop=False)
                            mm = pe.matmul(o, vs2[:, :, :], pn[:, b * 4:b * 4 + 4], start=False, stop=True)
                        mm.then_inc(S["s_o"], 1)

                    def down(q0, q1):
                        for q in range(q0, q1):
                            ch, ft = divmod(q, KT)
                            if q == 0:
                                pe.wait_ge(lo_done, count(g, ATT_S, ATT_S))
                            if ft == 0:
                                pe.wait_ge(S["heads_lo"], count(g, NB, min(NB, ((ch + 1) * CH - 1) // W + 1)))
                            if q == 2 * KT:
                                pe.wait_ge(S["s_ol"], ONE + 2 * g + 2)
                            if q >= 2:
                                pe.wait_ge(S["yadd"], count(g, DOWN_J, q - 1 if q < 2 * KT + 2 else q - 3))
                            down_job(pe, down_bank(q), 3, ft, ch, oh, ol).then_inc(jobs, 1)

                    for t in range(NB + 2):
                        if t <= NB:
                            project(t)
                        if t >= 1:
                            turn(t - 1)
                        if t >= 4:
                            values(t - 4)
                        if t >= 2:
                            scores(t - 2)
                        if t >= 3:
                            turn_probs(t - 3)
                    down(0, 4)
                    sample_scores()
                    down(4, 6)
                    values(NB - 2)
                    down(6, 8)
                    turn_probs(NB - 1)
                    sample_turn()
                    down(8, 12)
                    values(NB - 1)
                    sample_turn_probs()
                    down(12, 14)
                    sample_values()
                    down(14, DOWN_J)

            @block.scalar
            def _(act):
                with act.Fori(0, NG) as g:
                    def v_hi(b):
                        m = P if b < NB else NS
                        act.wait_ge(jobs, count(g, ATT_J, b + 1))
                        if b < NB:
                            act.wait_ge(S["heads"], count(g, NB, max(b - 4, 0)))
                            act.activation(vh[:, b % VR, :, :], bank[b % 2][:, 320:384].rearrange("m (a n) -> m a n", a=1)
                                           .to_broadcast([P, 2, HD]), ACT.Copy).then_inc(S["v_hi"], 1)
                        if b == NB - 1:
                            act.wait_ge(S["kv_out"], count(g, 64, 0))
                            act.activation(vf[:, 0, :], bank[b % 2][:, 320:384], ACT.Copy).then_inc(S["v_fp"], 1)
                        if b == NB:
                            act.wait_ge(S["s_o"], ONE + g)
                            act.activation(vs2[:, :, :], bank[b % 2][0:NS, 320:384].rearrange("m (a n) -> m a n", a=1)
                                           .to_broadcast([NS, 2, HD]), ACT.Copy).then_inc(S["v_fp"], 1)

                    def t_hi(b):
                        act.wait_ge(S["back"], count(g, NB + 1, b + 1))
                        if b < NB:
                            act.wait_ge(S["score"], count(g, NB, b))
                            act.activation(qh[:, :], bank[2][:, 0:256], ACT.Copy).then_inc(S["t_hi"], 1)
                            act.activation(kh[:, b % KR * W:(b % KR + 1) * W], bank[2][:, 256:384], ACT.Copy).then_inc(S["t_hi"], 1)

                    def exps(b):
                        act.wait_ge(S["small"], count(g, 3 * NB, 3 * b + 3))
                        k0 = 0 if b else W
                        act.wait_ge(S["pt"], count(g, NB, b))
                        for h in range(GH):
                            act.activation(prob[:, h, k0:], sm[:, h, k0:], ACT.Exp, bias=st[:, 2, h:h + 1],
                                           accum_out=st[:, 4, h:h + 1])
                        act.activation(st[:, 5, :], st[:, 3, :], ACT.Exp).then_inc(S["expd"], 1)

                    def pt_hi(b):
                        act.wait_ge(S["pt"], count(g, NB, b + 1))
                        act.wait_ge(S["heads"], count(g, NB, b))
                        for t in range(0 if b else 1, 2):
                            a = act.activation(pth[:, t, :], bank[5 + t][:, :], ACT.Copy)
                        a.then_inc(S["pt_hi"], 1)

                    def heads_hi(b):
                        act.wait_ge(S["heads"], count(g, NB, b + 1))
                        if b == 0:
                            act.wait_ge(jobs, count(g, ATT_J, 0))
                        for h in range(2):
                            r = slice(HD * h, HD * h + HD)
                            a = act.activation(oh[r, :, b * W:(b + 1) * W],
                                               bank[7][r, :].rearrange("p (j h n) -> p j h n", j=2, h=2)[:, :, h, :],
                                               ACT.Copy)
                        a.then_inc(S["heads_hi"], 1)

                    for t in range(NB + 2):
                        if t <= NB:
                            v_hi(t)
                        if t >= 1:
                            t_hi(t - 1)
                        if t >= 4:
                            heads_hi(t - 4)
                        if t >= 3:
                            pt_hi(t - 3)
                        if t >= 2:
                            exps(t - 2)
                    act.wait_ge(S["qk"], count(g, 2 * (NB + 1), 2 * (NB + 1)))
                    act.wait_ge(S["v_fp"], ONE + 2 * g + 2)
                    gg = bass.ds(g, 1)
                    act.dma_start(A["kwin_p"][:, gg, :].rearrange("t a d -> t (a d)"), qk[:, 1, 256:320]).then_inc(S["kv_out"], 16)
                    act.dma_start(A["vwin_p"][:, gg, :].rearrange("t a d -> t (a d)"), vf[:, 0, :]).then_inc(S["kv_out"], 16)
                    act.dma_start(A["kwin_s"][:, W - 1, gg, :].rearrange("t a d -> t (a d)"), qk[0:NS, 0, 256:320]).then_inc(S["kv_out"], 16)
                    act.dma_start(A["vwin_s"][:, W - 1, gg, :].rearrange("t a d -> t (a d)"), vs2[:, 0, :]).then_inc(S["kv_out"], 16)
                    split_hi(act, ATT_S, g, ATT_S)
                    heads_hi(NB - 2)
                    split_hi(act, ATT_S + 1, g, ATT_S)
                    pt_hi(NB - 1)
                    act.wait_ge(S["s_mx"], ONE + 3 * g + 3)
                    act.activation(sp_[:, :], bank[2][0:32, 0:W + 1], ACT.Exp, bias=sst[:, 2:3], scale=HD ** -0.5,
                                   accum_out=sst[:, 4:5])
                    act.activation(sst[:, 5:6], sst[:, 3:4], ACT.Exp).then_inc(S["s_ex"], 1)
                    heads_hi(NB - 1)
                    split_hi(act, ATT_S + 2, g, ATT_S)
                    act.wait_ge(S["s_o"], ONE + g + 1)
                    for h in range(2):
                        r = slice(HD * h, HD * h + HD)
                        act.activation(oh[r, :, SEQ:TOK],
                                       bank[2][r, 0:32].rearrange("p (b j h) -> p j h b", j=2, h=2)[:, :, h, :],
                                       ACT.Copy).then_inc(S["s_oh"], 1)
                    act.wait_ge(jobs, count(g, ATT_J, ATT_J))
                    for j in range(3, ATT_S):
                        split_hi(act, ATT_S + j, g, ATT_S)
                act.wait_ge(S["kv_out"], ONE + 64 * NG)

            @block.vector
            def _(dve):
                dve.wait_ge(S["table_in"], ONE + 16 * 6)
                with dve.Fori(0, NG) as g:
                    def rope(b):
                        m = P if b < NB else NS
                        if b < NB:
                            dve.wait_ge(S["v_hi"], count(g, NB, b + 1))
                        if b >= NB - 1:
                            dve.wait_ge(S["v_fp"], count(g, 2, b - NB + 2))
                        dve.wait_ge(S["qk"], count(g, 2 * (NB + 1), 2 * (b - 1)) if b >= 2 else count(g, 2 * (NB + 1), 0))
                        src = bank[b % 2][0:m, 0:320].rearrange("m (h a n) -> m h a n", h=5, a=2)
                        a1 = t1[0:m, b % 2, :].rearrange("m (h a n) -> m h a n", h=5, a=2)
                        a2 = t2[0:m, b % 2, :].rearrange("m (h a n) -> m h a n", h=5, a=2)
                        cs = cosT[0:m, b:b + 1, :].rearrange("m (a c) n -> m a c n", a=1)
                        sn = sinT[0:m, b, :].rearrange("m (a n) -> m a n", a=1)
                        dve.tensor_tensor(a1, src, cs.to_broadcast([m, 5, 2, 32]), ALU.mult)
                        dve.tensor_tensor(a2[:, :, 1, :], src[:, :, 0, :], sn.to_broadcast([m, 5, 32]), ALU.mult)
                        dve.scalar_tensor_tensor(a2[:, :, 0, :], src[:, :, 1, :], -1.0, sn.to_broadcast([m, 5, 32]),
                                                 ALU.mult, ALU.mult).then_inc(S["rope_t"], 1)
                        if b < NB:
                            dve.tensor_tensor(vl[:, b % VR, :, :], bank[b % 2][:, 320:384].rearrange("m (a n) -> m a n", a=1)
                                              .to_broadcast([P, 2, HD]), vh[:, b % VR, :, :].bitcast(F32),
                                              ALU.subtract).then_inc(S["v_free"], 1)

                    def t_lo(b):
                        if b < NB:
                            dve.wait_ge(S["t_hi"], count(g, 2 * NB, 2 * b + 2))
                            dve.tensor_tensor(ql[:, :], bank[2][:, 0:256], qh[:, :].bitcast(F32), ALU.subtract).then_inc(S["t_lo"], 1)
                            dve.tensor_tensor(kl[:, b % KR * W:(b % KR + 1) * W], bank[2][:, 256:384],
                                              kh[:, b % KR * W:(b % KR + 1) * W].bitcast(F32), ALU.subtract).then_inc(S["t_lo"], 1)
                        else:
                            dve.wait_ge(S["back"], count(g, NB + 1, NB + 1))
                            dve.tensor_copy(sq[:, :, :], bank[2][:, 0:384].rearrange("p (a n) -> p a n", a=3)[:, :, 0:NS])\
                               .then_inc(S["t_lo"], 1)

                    def shift(b):
                        dve.wait_ge(S["score"], count(g, NB, b + 1))
                        dve.wait_ge(S["expd"], count(g, NB, b))
                        k0 = 0 if b else W
                        dve.sem_inc(S["passed"], 1)
                        for h in range(GH):
                            dve.tensor_tensor_reduce(out=sm[:, h, k0:], in0=bank[3 + h % 2][:, (h // 2) * 256 + k0:(h // 2) * 256 + 256],
                                                     in1=mask[:, k0:], scale=HD ** -0.5, scalar=LN_BIG, op0=ALU.add,
                                                     op1=ALU.max, accum_out=st[:, 0, h:h + 1]).then_inc(S["shifted"], 1)
                        dve.wait_ge(S["shifted"], count(g, GH * NB, GH * b + GH))
                        sk = sinkb[:, bass.ds(g * GH, GH)]
                        dve.tensor_tensor(st[:, 1, :], st[:, 0, :], sk, ALU.max).then_inc(S["small"], 1)
                        dve.wait_ge(S["small"], count(g, 3 * NB, 3 * b + 1))
                        dve.tensor_scalar(st[:, 2, :], st[:, 1, :], -1.0, None, ALU.mult).then_inc(S["small"], 1)
                        dve.tensor_tensor(st[:, 3, :], sk, st[:, 1, :], ALU.subtract).then_inc(S["small"], 1)

                    def inverse(b):
                        dve.wait_ge(S["expd"], count(g, NB, b + 1))
                        dve.wait_ge(S["probs"], count(g, NB, b))
                        dve.tensor_tensor(st[:, 6, :], st[:, 4, :], st[:, 5, :], ALU.add).then_inc(S["small2"], 1)
                        dve.wait_ge(S["small2"], count(g, NB, b + 1))
                        dve.reciprocal(st[:, 7, :], st[:, 6, :]).then_inc(S["inv"], 1)

                    def pt_lo(b):
                        dve.wait_ge(S["pt_hi"], count(g, NB, b + 1))
                        for t in range(0 if b else 1, 2):
                            a = dve.tensor_tensor(ptl[:, t, :], bank[5 + t][:, :], pth[:, t, :].bitcast(F32), ALU.subtract)
                        a.then_inc(S["pt_lo"], 1)

                    def heads_lo(b):
                        dve.wait_ge(S["heads_hi"], count(g, NB, b + 1))
                        for h in range(2):
                            r = slice(HD * h, HD * h + HD)
                            a = dve.tensor_tensor(ol[r, :, b * W:(b + 1) * W],
                                                  bank[7][r, :].rearrange("p (j h n) -> p j h n", j=2, h=2)[:, :, h, :],
                                                  oh[r, :, b * W:(b + 1) * W].bitcast(F32), ALU.subtract)
                        a.then_inc(S["heads_lo"], 1)

                    def sample_copy():
                        dve.wait_ge(S["s_sc"], ONE + g + 1)
                        for n in range(2):
                            dve.tensor_copy(ss[:, n:32:2], bank[3 + n][:, n:32:2]).then_inc(S["s_scc"], 1)
                            dve.tensor_copy(row[:, n:32:2], bank[3 + n][0:1, 32 + n:64:2]).then_inc(S["s_scc"], 1)

                    def sample_shift():
                        dve.wait_ge(S["s_tr"], ONE + g + 1)
                        dve.reduce_max(sst[:, 0:1], bank[2][0:32, 0:W + 1], AXX).then_inc(S["dchain"], 1)
                        dve.wait_ge(S["dchain"], count(g, 4, 1))
                        skc = sinkc[:, bass.ds(g, 1)]
                        dve.tensor_scalar(sst[:, 1:2], sst[:, 0:1], HD ** -0.5, skc, ALU.mult, ALU.max).then_inc(S["s_mx"], 1)
                        dve.wait_ge(S["s_mx"], count(g, 3, 1))
                        dve.tensor_scalar(sst[:, 2:3], sst[:, 1:2], -1.0, None, ALU.mult).then_inc(S["s_mx"], 1)
                        dve.tensor_tensor(sst[:, 3:4], skc, sst[:, 1:2], ALU.subtract).then_inc(S["s_mx"], 1)

                    def sample_probs():
                        dve.wait_ge(S["s_ex"], ONE + g + 1)
                        dve.tensor_tensor(sst[:, 6:7], sst[:, 4:5], sst[:, 5:6], ALU.add).then_inc(S["dchain"], 1)
                        dve.wait_ge(S["dchain"], count(g, 4, 2))
                        dve.reciprocal(sst[:, 7:8], sst[:, 6:7]).then_inc(S["dchain"], 1)
                        dve.wait_ge(S["dchain"], count(g, 4, 3))
                        dve.tensor_scalar(sp_[:, :], sp_[:, :], sst[:, 7:8], None, ALU.mult).then_inc(S["dchain"], 1)
                        dve.wait_ge(S["dchain"], count(g, 4, 4))
                        dve.tensor_scalar(dg[:, :], ident[0:32, 0:32], sp_[:, W:W + 1], None, ALU.mult).then_inc(S["s_p"], 1)

                    def sample_probs_copy():
                        dve.wait_ge(S["s_pt"], ONE + g + 1)
                        dve.tensor_copy(spt[:, :], bank[5][:, 0:32]).then_inc(S["s_ptc"], 1)
                        dve.tensor_copy(pn[:, :], bank[6][0:NS, 0:32]).then_inc(S["s_ptc"], 1)

                    def sample_heads_lo():
                        dve.wait_ge(S["s_oh"], ONE + 2 * g + 2)
                        for h in range(2):
                            r = slice(HD * h, HD * h + HD)
                            dve.tensor_tensor(ol[r, :, SEQ:TOK],
                                              bank[2][r, 0:32].rearrange("p (b j h) -> p j h b", j=2, h=2)[:, :, h, :],
                                              oh[r, :, SEQ:TOK].bitcast(F32), ALU.subtract).then_inc(S["s_ol"], 1)

                    def add_y(q0, q1):
                        for q in range(q0, q1):
                            ch, ft = divmod(q, KT)
                            dve.wait_ge(jobs, count(g, ATT_J, NB + 2 + q))
                            dve.tensor_tensor(y[:, ft, columns(ch)], down_bank(q), y[:, ft, columns(ch)],
                                              ALU.add).then_inc(S["yadd"], 1)

                    for t in range(NB + 2):
                        if t >= 3:
                            inverse(t - 3)
                        if t <= NB:
                            rope(t)
                        if t >= 1:
                            t_lo(t - 1)
                        if t >= 2:
                            shift(t - 2)
                        if t >= 3:
                            pt_lo(t - 3)
                        if t >= 4:
                            heads_lo(t - 4)
                    add_y(0, 4)
                    inverse(NB - 1)
                    sample_copy()
                    add_y(4, 6)
                    heads_lo(NB - 2)
                    add_y(6, 8)
                    pt_lo(NB - 1)
                    sample_shift()
                    add_y(8, 12)
                    sample_probs()
                    heads_lo(NB - 1)
                    sample_probs_copy()
                    add_y(12, 14)
                    sample_heads_lo()
                    add_y(14, DOWN_J)

            @block.gpsimd
            def _(pool):
                with pool.Fori(0, NG) as g:
                    def add_rope(b):
                        m = P if b < NB else NS
                        pool.wait_ge(S["rope_t"], count(g, NB + 1, b + 1))
                        pool.wait_ge(S["back"], count(g, NB + 1, max(b - 1, 0)))
                        if b == 0 or b == 1:
                            pool.wait_ge(S["kv_out"], count(g, 64, 0))
                        pool.tensor_tensor(qk[0:m, b % 2, 0:256], t1[0:m, b % 2, 0:256], t2[0:m, b % 2, 0:256],
                                           ALU.add).then_inc(S["qk"], 1)
                        def twice(t):
                            return t[0:m, b % 2, 256:320].rearrange("m (a n) -> m a n", a=1).to_broadcast([m, 2, HD])
                        pool.tensor_tensor(qk[0:m, b % 2, 256:384].rearrange("m (a n) -> m a n", a=2), twice(t1), twice(t2),
                                           ALU.add).then_inc(S["qk"], 1)

                    def probs(b):
                        pool.wait_ge(S["inv"], count(g, NB, b + 1))
                        k0 = 0 if b else W
                        pool.tensor_tensor(prob[:, :, k0:], prob[:, :, k0:],
                                           st[:, 7, :].rearrange("p (h a) -> p h a", a=1).to_broadcast([P, GH, 2 * W - k0]),
                                           ALU.mult).then_inc(S["probs"], 1)

                    for t in range(NB + 3):
                        if t >= 3:
                            probs(t - 3)
                        if t <= NB:
                            add_rope(t)
                    for j in range(3):
                        split_lo(pool, ATT_S + j, g, ATT_S)
                    pool.wait_ge(jobs, count(g, ATT_J, ATT_J))
                    for j in range(3, ATT_S):
                        split_lo(pool, ATT_S + j, g, ATT_S)


def layer_norm(nc, A, env, layer, which, more):
    ctx, sem, bank = env["ctx"], env["sem"], env["bank"]
    xh, xl, y, ones, columns = env["xh"], env["xl"], env["y"], env["ones"], env["columns"]
    nm = f"n{layer}{which}_"
    S = env["S_ln"]
    past = {n: (2 * layer + (which == "ffn")) * k for n, k in LN_COUNTS.items()}
    with ExitStack() as c:
        def sb(name, shape, dt=F32):
            return c.enter_context(nc.sbuf_tensor(nm + name, shape, dt))
        gb = sb("gb", [P, 2, KT])
        ab = sb("ab", [P, KT])
        sq = sb("sq", [P, NCH, KT, CH])
        rs = sb("rs", [P, NCH, CH])

        with nc.Block() as block:
            @block.sync
            def _(sp):
                sp.dma_start(gb[:, :, :], A[f"ln_{which}"][layer]).then_inc(S["in_"], 16)
                if not more:
                    for ch in range(NCH):
                        sp.wait_ge(S["shift"], ONE + ch + 1 + past["shift"])
                        sp.dma_start(A["y"][:, :, columns(ch)], y[:, :, columns(ch)]).then_inc(S["out"], 16)
                    sp.wait_ge(S["out"], ONE + 16 * NCH + past["out"])

            @block.tensor
            def _(pe):
                def mean(ch):
                    for k in range(KT):
                        mm = pe.matmul(bank[ch][:, 0:CH], ones[:, :], y[:, k, columns(ch)], start=(k == 0), stop=(k == KT - 1))
                    mm.then_inc(S["mean"], 1)

                def var(ch):
                    pe.wait_ge(S["squares"], ONE + ch + 1 + past["squares"])
                    for k in range(KT):
                        mm = pe.matmul(bank[3 + ch][:, 0:CH], ones[:, :], sq[:, ch, k, :], start=(k == 0), stop=(k == KT - 1))
                    mm.then_inc(S["var"], 1)

                for ch in range(NCH):
                    mean(ch)
                for ch in range(NCH):
                    var(ch)

            @block.scalar
            def _(act):
                def root(ch):
                    act.wait_ge(S["eps"], ONE + ch + 1 + past["eps"])
                    act.activation(rs[:, ch, :], rs[:, ch, :], ACT.Sqrt).then_inc(S["std"], 1)

                def hi(ch):
                    act.wait_ge(S["scaled"], ONE + ch + 1 + past["scaled"])
                    for k in range(KT):
                        a = act.activation(xh[:, k, columns(ch)], y[:, k, columns(ch)], ACT.Identity, bias=gb[:, 1, k:k + 1])
                    a.then_inc(S["hi"], 1)

                def shift(ch):
                    if more:
                        act.wait_ge(S["lo"], ONE + ch + 1 + past["lo"])
                    else:
                        act.wait_ge(S["scaled"], ONE + ch + 1 + past["scaled"])
                    for k in range(KT if ch < NCH - 1 or not more else KT // 2):
                        a = act.activation(y[:, k, columns(ch)], y[:, k, columns(ch)], ACT.Identity,
                                           bias=ab[:, k:k + 1] if more else gb[:, 1, k:k + 1], scale=ALPHA if more else 1.0)
                    a.then_inc(S["shift"], 1)

                for ch in range(NCH):
                    act.wait_ge(S["centred"], ONE + ch + 1 + past["centred"])
                    act.activation(sq[:, ch, :, :], y[:, :, columns(ch)], ACT.Square).then_inc(S["squares"], 1)
                root(0)
                root(1)
                act.wait_ge(S["in_"], ONE + 16 + past["in_"])
                act.wait_ge(S["bias"], ONE + 1 + past["bias"])
                for ch in range(NCH):
                    if ch == NCH - 2:
                        root(NCH - 1)
                    if more:
                        hi(ch)
                    if ch:
                        shift(ch - 1)
                shift(NCH - 1)

            @block.vector
            def _(dve):
                dve.wait_ge(S["in_"], ONE + 16 + past["in_"])

                def every(t):
                    return t.rearrange("p (a n) -> p a n", a=1).to_broadcast([P, KT, CH])

                def centre(ch):
                    dve.wait_ge(S["mean"], ONE + ch + 1 + past["mean"])
                    dve.tensor_tensor(y[:, :, columns(ch)], y[:, :, columns(ch)], every(bank[ch][:, 0:CH]),
                                      ALU.subtract).then_inc(S["centred"], 1)

                def eps(ch):
                    dve.wait_ge(S["var"], ONE + ch + 1 + past["var"])
                    dve.tensor_scalar(rs[:, ch, :], bank[3 + ch][:, 0:CH], EPS, None, ALU.add).then_inc(S["eps"], 1)

                def inverse(ch):
                    dve.wait_ge(S["std"], ONE + ch + 1 + past["std"])
                    dve.reciprocal(rs[:, ch, :], rs[:, ch, :]).then_inc(S["inv"], 1)

                def scale(ch):
                    dve.wait_ge(S["inv"], ONE + ch + 1 + past["inv"])
                    for k in range(KT):
                        a = dve.scalar_tensor_tensor(y[:, k, columns(ch)], y[:, k, columns(ch)], gb[:, 0, k:k + 1],
                                                     rs[:, ch, :], ALU.mult, ALU.mult)
                    a.then_inc(S["scaled"], 1)

                def shift(ch, k0):
                    dve.wait_ge(S["lo"], ONE + ch + 1 + past["lo"])
                    dve.wait_ge(S["bias"], ONE + 1 + past["bias"])
                    for k in range(k0, KT):
                        dve.tensor_scalar(y[:, k, columns(ch)], y[:, k, columns(ch)], ALPHA, ab[:, k:k + 1], ALU.mult, ALU.add)

                def lo(ch):
                    dve.wait_ge(S["hi"], ONE + ch + 1 + past["hi"])
                    for k in range(KT):
                        a = dve.scalar_tensor_tensor(xl[:, k, columns(ch)], y[:, k, columns(ch)], gb[:, 1, k:k + 1],
                                                     xh[:, k, columns(ch)].bitcast(F32), ALU.add, ALU.subtract)
                    a.then_inc(S["lo"], 1)

                for ch in range(NCH):
                    centre(ch)
                dve.tensor_scalar(ab[:, :], gb[:, 1, :], ALPHA, None, ALU.mult).then_inc(S["bias"], 1)
                eps(0)
                inverse(0)
                for ch in range(NCH):
                    if ch < NCH - 1:
                        eps(ch + 1)
                    scale(ch)
                    if ch < NCH - 1:
                        inverse(ch + 1)
                    if more and ch:
                        lo(ch - 1)
                if more:
                    lo(NCH - 1)
                    shift(NCH - 1, KT // 2)


def conv_ffn(nc, A, env, layer):
    ctx, sem, bank, plus, count = env["ctx"], env["sem"], env["bank"], env["plus"], env["count"]
    y = env["y"]
    jobs, lo_done = env["jobs"], env["lo_done"]
    load_slab, split_hi, split_lo = env["load_slab"], env["split_hi"], env["split_lo"]
    columns, up_job, down_job = env["columns"], env["up_job"], env["down_job"]
    s0, j0 = (S_FFN0, J_FFN0) if layer == 0 else (S_FFN1, J_FFN1)
    nm = f"f{layer}_"
    S = {n: sem(nm + n) for n in SEMS[nm]}
    IT = UP_J + DOWN_J
    LOOPS = (NBLK - 1) // 2 - layer

    with ExitStack() as c:
        def sb(name, shape, dt=F32):
            return c.enter_context(nc.sbuf_tensor(nm + name, shape, dt))
        ab = sb("ab", [P, TOK + 2])
        cv = sb("cv", [P, TOK])
        hf = sb("hf", [P, TOK])
        hh = sb("hh", [P, 2, 2, TOK], F32R)
        hl = sb("hl", [P, 2, 2, TOK], F32R)
        taps = sb("taps", [P, FT * 4])
        past = sb("past", [P, FT, 2, NS])
        cout = sb("cout", [P, FT * 10])

        with nc.Block() as block:
            @block.sync
            def _(sp):
                sp.dma_start(taps[:, :], A["taps"][layer]).then_inc(S["in_"], 16)
                sp.dma_start(past[:, :, :, :], A["past"][layer]).then_inc(S["in_"], 16)
                first = s0 + AHEAD
                n = min(FFN_N, N_SLABS - first)
                with sp.Fori(0, n // 12) as i:
                    for j in range(12):
                        load_slab(sp, first + j, i, 12)
                for j in range(n // 12 * 12, n):
                    load_slab(sp, first + j)
                sp.wait_ge(S["conv"], ONE + FT * 4)
                sp.dma_start(A["conv_rows"][layer], cout[:, :]).then_inc(S["out"], 16)
                sp.dma_start(A["conv_past"][layer], past[:, :, 1, :]).then_inc(S["out"], 16)
                sp.wait_ge(S["out"], ONE + 32)

            @block.tensor
            def _(pe):
                def up(n, i=0):
                    m = (6 * n - 2) + s0 if n else s0
                    for t in range(2):
                        for kind in range(2):
                            s = m + 2 * t + kind
                            per = 12 if n else 0
                            pe.wait_ge(lo_done, count(i, per, s + 1))
                            for ch in range(NCH):
                                before = 6 * n + 3 * t + ch - 2
                                done = S["a_in"] if kind == 0 else S["gate"]
                                if before > 0:
                                    pe.wait_ge(done, count(i, per, before))
                                if t == 0 and kind == 0 and n >= 1 and ch < 2:
                                    pe.wait_ge(S["yadd"], count(i, 2 * DOWN_J, DOWN_J * (n - 1)))
                                up_job(pe, bank[3 * kind + ch][:, 0:CH], s, ch).then_inc(jobs, 1)

                def down(n, i=0, loop=True):
                    s = s0 + 8 + 6 * n if n < NBLK - 1 else s0 + FFN_N - 2
                    per = 12 if loop else 0
                    pe.wait_ge(lo_done, count(i, per, s + 2))
                    pe.wait_ge(S["h_lo"], count(i, 4 if loop else 0, 2 * n + 2))
                    for q in range(DOWN_J):
                        ft, ch = divmod(q, NCH)
                        if q < 2:
                            if n < NBLK - 1:
                                if n >= 1 or loop:
                                    if n >= 1:
                                        pe.wait_ge(S["yadd"], count(i, 2 * DOWN_J if loop else 0, DOWN_J * n - 3 + q))
                                    else:
                                        pe.wait_ge(S["yadd"], count(i, 2 * DOWN_J, 0))
                            else:
                                pe.wait_ge(S["yadd"], ONE + DOWN_J * n - 3 + q)
                        elif q < 4:
                            if n < NBLK - 1:
                                pe.wait_ge(S["a_in"], count(i, 12 if loop else 0, 6 * (n + 1) + 3 + q - 1))
                            else:
                                pe.wait_ge(S["yadd"], ONE + DOWN_J * n - 3 + q)
                        else:
                            pe.wait_ge(S["yadd"], count(i, 2 * DOWN_J if loop else 0, DOWN_J * n + q - 3))
                        b = (6, 7, 0, 1)[q % 4]
                        down_job(pe, bank[b][:, 0:CH], s, ft, ch, hh[:, n % 2, :, :], hl[:, n % 2, :, :]).then_inc(jobs, 1)

                pe.wait_ge(S["in_"], ONE + 32)
                up(0)
                with pe.Fori(0, LOOPS) as i:
                    for n in range(2):
                        up(n + 1, i)
                        down(n, i)
                for i in range(LOOPS, (NBLK - 1) // 2):
                    for n in range(2):
                        up(n + 1, i)
                        down(n, i)
                down(NBLK - 1, loop=False)

            def ju(n):
                return j0 + (UP_J + (n - 1) * IT if n else 0)

            def jd(n):
                return j0 + UP_J + n * IT + (UP_J if n < NBLK - 1 else 0)

            @block.scalar
            def _(act):
                def up(n, i=0):
                    per = 1 if n else 0
                    s = s0 + (6 * n - 2 if n else 0)
                    for t in range(2):
                        for ch in range(NCH):
                            act.wait_ge(jobs, count(i, 2 * IT * per, ju(n) + 6 * t + ch + 1))
                            if ch == 0 and (n or t):
                                act.wait_ge(S["conv"], count(i, 16 * per, 4 * (2 * n + t)))
                            act.activation(ab[:, 2 + ch * CH:2 + (ch + 1) * CH], bank[ch][:, 0:CH],
                                           ACT.Copy).then_inc(S["a_in"], 1)
                        split_hi(act, s + 2 * t + AHEAD, i, 12 * per)
                        act.wait_ge(S["conv"], count(i, 16 * per, 4 * (2 * n + t) + 4))
                        act.activation(cv[:, :], cv[:, :], ACT.Silu).then_inc(S["silu"], 1)
                        split_hi(act, s + 2 * t + 1 + AHEAD, i, 12 * per)
                        act.wait_ge(S["gate"], count(i, 12 * per, 3 * (2 * n + t) + 3))
                        if n >= 2:
                            act.wait_ge(jobs, count(i, 2 * IT * per, jd(n - 2) + DOWN_J))
                        act.activation(hh[:, n % 2, t, :], hf[:, :], ACT.Copy).then_inc(S["h_hi"], 1)

                def down(n, i=0, loop=True):
                    s = s0 + 8 + 6 * n if n < NBLK - 1 else s0 + FFN_N - 2
                    per = 12 if loop else 0
                    for j in range(2):
                        split_hi(act, s + j + AHEAD, i, per)

                act.wait_ge(S["in_"], ONE + 32)
                act.wait_ge(S["border"], ONE + 1)
                up(0)
                with act.Fori(0, LOOPS) as i:
                    for n in range(2):
                        up(n + 1, i)
                        down(n, i)
                for i in range(LOOPS, (NBLK - 1) // 2):
                    for n in range(2):
                        up(n + 1, i)
                        down(n, i)
                down(NBLK - 1, loop=False)

            @block.vector
            def _(dve):
                def up(n, i=0):
                    per = 1 if n else 0
                    s = s0 + (6 * n - 2 if n else 0)
                    for t in range(2):
                        tile = 2 * n + t
                        at = plus(i, 4 * per, tile)

                        def tap(q):
                            return taps[:, 4 * tile + q:4 * tile + q + 1] if not per else taps[:, bass.ds(at * 4 + q, 1)]

                        def before(q):
                            if not per:
                                return past[:, tile, q, :]
                            return past[:, bass.ds(at, 1), q, :].rearrange("p a b -> p (a b)")
                        last = plus(i, 12 * per, 3 * (2 * n + t) + 3)
                        dve.wait_ge(S["a_in"], ONE + last)
                        if n or t:
                            dve.wait_ge(S["gate"], count(i, 12 * per, 3 * (2 * n + t)))
                        at4 = plus(i, 16 * per, 4 * (2 * n + t))
                        dve.tensor_scalar(cv[:, 0:SEQ], ab[:, 0:SEQ], tap(0), tap(3), ALU.mult, ALU.add)
                        dve.tensor_scalar(cv[:, SEQ:TOK], before(0), tap(0), tap(3), ALU.mult, ALU.add).then_inc(S["conv"], 1)
                        dve.wait_ge(S["conv"], ONE + at4 + 1)
                        dve.scalar_tensor_tensor(cv[:, 0:SEQ], ab[:, 1:SEQ + 1], tap(1), cv[:, 0:SEQ], ALU.mult, ALU.add)
                        dve.scalar_tensor_tensor(cv[:, SEQ:TOK], before(1), tap(1), cv[:, SEQ:TOK], ALU.mult,
                                                 ALU.add).then_inc(S["conv"], 1)
                        dve.wait_ge(S["conv"], ONE + at4 + 2)
                        dve.scalar_tensor_tensor(cv[:, :], ab[:, 2:TOK + 2], tap(2), cv[:, :], ALU.mult, ALU.add).then_inc(S["conv"], 1)
                        keep = cout[:, 10 * tile:10 * tile + 10] if not per else cout[:, bass.ds(at * 10, 10)]
                        dve.tensor_copy(keep, ab[:, SEQ:TOK + 2]).then_inc(S["conv"], 1)
                        split_lo(dve, s + 2 * t + AHEAD, i, 12 * per)
                        dve.wait_ge(S["silu"], count(i, 4 * per, 2 * n + t + 1))
                        for ch in range(NCH):
                            dve.wait_ge(jobs, count(i, 2 * IT * per, ju(n) + 6 * t + 3 + ch + 1))
                            if ch == 0 and (n or t):
                                dve.wait_ge(S["h_lo"], count(i, 4 * per, 2 * n + t))
                            dve.tensor_tensor(hf[:, columns(ch)], cv[:, columns(ch)], bank[3 + ch][:, 0:CH],
                                              ALU.mult).then_inc(S["gate"], 1)
                        split_lo(dve, s + 2 * t + 1 + AHEAD, i, 12 * per)

                def down(n, i=0, loop=True):
                    s = s0 + 8 + 6 * n if n < NBLK - 1 else s0 + FFN_N - 2
                    per = 12 if loop else 0
                    for q in range(DOWN_J):
                        ft, ch = divmod(q, NCH)
                        b = (6, 7, 0, 1)[q % 4]
                        dve.wait_ge(jobs, count(i, 2 * IT if loop else 0, jd(n) + q + 1))
                        dve.tensor_tensor(y[:, ft, columns(ch)], bank[b][:, 0:CH], y[:, ft, columns(ch)],
                                          ALU.add).then_inc(S["yadd"], 1)
                    for j in range(2):
                        split_lo(dve, s + j + AHEAD, i, per)

                dve.memset(ab[:, 0:2], 0.0).then_inc(S["border"], 1)
                dve.wait_ge(S["border"], ONE + 1)
                dve.wait_ge(S["in_"], ONE + 32)
                up(0)
                with dve.Fori(0, LOOPS) as i:
                    for n in range(2):
                        up(n + 1, i)
                        down(n, i)
                for i in range(LOOPS, (NBLK - 1) // 2):
                    for n in range(2):
                        up(n + 1, i)
                        down(n, i)
                down(NBLK - 1, loop=False)

            @block.gpsimd
            def _(pool):
                def up(n, i=0):
                    per = 1 if n else 0
                    for t in range(2):
                        pool.wait_ge(S["h_hi"], count(i, 4 * per, 2 * n + t + 1))
                        pool.tensor_tensor(hl[:, n % 2, t, :], hf[:, :], hh[:, n % 2, t, :].bitcast(F32),
                                           ALU.subtract).then_inc(S["h_lo"], 1)

                up(0)
                with pool.Fori(0, LOOPS) as i:
                    for n in range(2):
                        up(n + 1, i)
                for i in range(LOOPS, (NBLK - 1) // 2):
                    for n in range(2):
                        up(n + 1, i)


def retention_in(nc, A, env):
    ctx, sem, bank, plus, count = env["ctx"], env["sem"], env["bank"], env["plus"], env["count"]
    jobs, lo_done = env["jobs"], env["lo_done"]
    load_slab, split_hi, split_lo = env["load_slab"], env["split_hi"], env["split_lo"]
    columns, up_job = env["columns"], env["up_job"]
    S = {n: sem("p_" + n) for n in SEMS["p_"]}
    NT = 12
    TJ = NT * NCH
    with ExitStack() as c:
        def sb(name, shape, dt=F32):
            return c.enter_context(nc.sbuf_tensor("p_" + name, shape, dt))
        cosR = sb("cosR", [P, TOK])
        sinR = sb("sinR", [P, TOK])
        prod = sb("prod", [P, 4, TOK])
        rot = sb("rot", [P, 2, TOK])
        plain = sb("plain", [P, 2, TOK])

        with nc.Block() as block:
            @block.sync
            def _(sp):
                sp.dma_start(cosR[:, :], A["cosR"]).then_inc(S["in_"], 16)
                sp.dma_start(sinR[:, :], A["sinR"]).then_inc(S["in_"], 16)
                with sp.Fori(0, RH) as h:
                    for j in range(NT):
                        load_slab(sp, S_RIN + AHEAD + j, h, NT)

            @block.tensor
            def _(pe):
                with pe.Fori(0, RH) as h:
                    for j in range(NT):
                        pe.wait_ge(lo_done, count(h, NT, S_RIN + j + 1))
                        for ch in range(NCH):
                            b = 3 * (j % 2) + ch
                            if j < 2:
                                pe.wait_ge(S["plain"], count(h, 24, 0))
                            elif j < 4:
                                pe.wait_ge(S["prod"], count(h, 24, 4 * (ch + 1)))
                            elif j < 6:
                                pe.wait_ge(S["prod"], count(h, 24, 12 + 4 * (ch + 1)))
                            else:
                                pe.wait_ge(S["plain"], count(h, 24, 3 * (j - 6) + ch + 1))
                            up_job(pe, bank[b][:, 0:CH], S_RIN + j, ch).then_inc(jobs, 1)

            @block.scalar
            def _(act):
                with act.Fori(0, RH) as h:
                    for j in range(NT):
                        if j >= 4:
                            for ch in range(NCH):
                                act.wait_ge(jobs, count(h, TJ, J_RIN + 3 * j + ch + 1))
                                if ch == 0:
                                    n = j - 4
                                    act.wait_ge(S[f"out_p{n % 2}"], count(h, 64, 16 * (n // 2)))
                                act.activation(plain[:, j % 2, columns(ch)], bank[3 * (j % 2) + ch][:, 0:CH],
                                               ACT.Copy if j < 8 else ACT.Silu).then_inc(S["plain"], 1)
                            act.wait_ge(S["plain"], count(h, 24, 3 * (j - 4) + 3))
                            act.dma_start(A["scr"][bass.ds(h * NT + j, 1)].rearrange("a p n -> p (a n)"),
                                          plain[:, j % 2, :]).then_inc(S[f"out_p{j % 2}"], 16)
                        elif j % 2:
                            act.wait_ge(S["rot"], count(h, 4, j + 1))
                            for e in range(2):
                                act.dma_start(A["scr"][bass.ds(h * NT + j - 1 + e, 1)].rearrange("a p n -> p (a n)"),
                                              rot[:, e, :]).then_inc(S["out_r"], 16)
                        split_hi(act, S_RIN + j + AHEAD, h, NT)
                act.wait_ge(S["out_p0"], ONE + 16 * 4 * RH)
                act.wait_ge(S["out_p1"], ONE + 16 * 4 * RH)
                act.wait_ge(S["out_r"], ONE + 16 * 4 * RH)

            @block.vector
            def _(dve):
                dve.wait_ge(S["in_"], ONE + 32)
                with dve.Fori(0, RH) as h:
                    for j in range(NT):
                        if j in (1, 3):
                            for ch in range(NCH):
                                dve.wait_ge(jobs, count(h, TJ, J_RIN + 3 * j + ch + 1))
                                if ch == 0:
                                    dve.wait_ge(S["rot"], count(h, 4, j - 1))
                                t = columns(ch)
                                e, o = bank[ch][:, 0:CH], bank[3 + ch][:, 0:CH]
                                dve.tensor_tensor(prod[:, 0, t], e, cosR[:, t], ALU.mult).then_inc(S["prod"], 1)
                                dve.tensor_tensor(prod[:, 1, t], o, sinR[:, t], ALU.mult).then_inc(S["prod"], 1)
                                dve.tensor_tensor(prod[:, 2, t], o, cosR[:, t], ALU.mult).then_inc(S["prod"], 1)
                                dve.tensor_tensor(prod[:, 3, t], e, sinR[:, t], ALU.mult).then_inc(S["prod"], 1)
                        split_lo(dve, S_RIN + j + AHEAD, h, NT)

            @block.gpsimd
            def _(pool):
                with pool.Fori(0, RH) as h:
                    for pair in range(2):
                        pool.wait_ge(S["prod"], count(h, 24, 12 * (pair + 1)))
                        pool.wait_ge(S["out_r"], count(h, 64, 32 * pair))
                        pool.tensor_tensor(rot[:, 0, :], prod[:, 0, :], prod[:, 1, :], ALU.subtract).then_inc(S["rot"], 1)
                        pool.tensor_tensor(rot[:, 1, :], prod[:, 2, :], prod[:, 3, :], ALU.add).then_inc(S["rot"], 1)


def retention_core(nc, A, env):
    ctx, sem, bank, plus, count = env["ctx"], env["sem"], env["bank"], env["plus"], env["count"]
    ident, accumulate = env["ident"], env["accumulate"]
    S = {n: sem("r_" + n) for n in SEMS["r_"]}
    NT = 12
    with ExitStack() as c:
        def sb(name, shape, dt=F32):
            return c.enter_context(nc.sbuf_tensor("r_" + name, shape, dt))
        dec = sb("dec", [P, W + 5])
        m8 = sb("m8", [P, NS, NS])
        cx = sb("cx", [P, 2, NT, W])
        qkh = sb("qkh", [P, 2, 4, W], F32R)
        qkl = sb("qkl", [P, 2, 4, W], F32R)
        kdh = sb("kdh", [P, RK], F32R)
        kdl = sb("kdl", [P, RK], F32R)
        vh = sb("vh", [P, 2, RV], F32R)
        vl = sb("vl", [P, 2, RV], F32R)
        gt = sb("gt", [P, 2, RV])
        inn = sb("inn", [P, W])
        ih = sb("ih", [P, 2, W], F32R)
        il = sb("il", [P, 2, W], F32R)
        st6 = sb("st6", [P, 6])
        st = sb("st", [P, 8])
        ga = sb("ga", [P, RV])
        ob = sb("ob", [P, 4, W])
        state = [sb("state", [P, 2, RV])[:, :, :], env["raw"][:, 2, :].rearrange("p (e n) -> p e n", e=2)]
        sh = sb("sh", [P, 2, RV], F32R)
        sl = sb("sl", [P, 2, RV], F32R)
        xs = sb("xs", [P, NT, NS])
        xv = sb("xv", [NS, RV])
        xg = sb("xg", [NS, RV])
        qm = sb("qm", [P, 2, NS, NS])
        k16 = sb("k16", [P, 2, NS])
        s0 = env["raw"][:, 0:2, :].rearrange("p b (e n) -> p b e n", e=2)
        xst6 = sb("xst6", [NS, 6])
        xst = sb("xst", [NS, 8])
        xga = sb("xga", [NS, RV])
        xo = sb("xo", [P, 4, NS])

        kT, vT, gT, uB, kvB, sB, oT, xB = bank[0], bank[1], bank[2], bank[3], bank[4], bank[5], bank[6], bank[7]

        with nc.Block() as block:
            @block.sync
            def _(sp):
                sp.dma_start(m8[:, :, :], A["m8"]).then_inc(S["in_"], 16)
                sp.wait_ge(S["in_"], ONE + 16)
                with sp.Fori(0, RH) as h:
                    sp.wait_ge(S["s_lo"], count(h, NB, 0))
                    sp.sem_inc(S["passed"], 1)
                    sp.wait_ge(S["x_small"], count(h, 4, 0))
                    sp.sem_inc(S["passed"], 1)
                    sp.dma_start(dec[:, :], A["dec"][bass.ds(h, 1)].rearrange("a p n -> p (a n)")).then_inc(S["head_in"], 16)
                    for n in range(NB):
                        sp.wait_ge(S["turned"], count(h, NB, max(n - 1, 0)))
                        sp.sem_inc(S["passed"], 1)
                        sp.wait_ge(S["q_lo"], count(h, NB, max(n - 1, 0)))
                        sp.sem_inc(S["passed"], 1)
                        sp.dma_start(cx[:, n % 2, :, :],
                                     A["scr"][bass.ds(h * NT, NT)].rearrange("a p n -> p a n")[:, :, n * W:(n + 1) * W])\
                          .then_inc(S[f"qkvg{n % 2}"], 16)
                        if n == 0:
                            sp.wait_ge(S["x_o"], count(h, NS, 0))
                            sp.sem_inc(S["passed"], 1)
                            sp.wait_ge(S["x_mask"], count(h, 2, 0))
                            sp.sem_inc(S["passed"], 1)
                            sp.dma_start(xs[:, :, :], A["scr"][bass.ds(h * NT, NT)].rearrange("a p n -> p a n")[:, :, SEQ:TOK])\
                              .then_inc(S["x_in"], 16)
                        sp.wait_ge(S[f"st_out{n % 2}"], count(h, 8 * NS, 16 * (n // 2)))
                        sp.sem_inc(S["passed"], 1)
                        sp.wait_ge(S["x_o"], count(h, NS, max(n - 1, 0)))
                        sp.sem_inc(S["passed"], 1)
                        sp.dma_start(s0[:, n % 2, :, :], A["state_in"][n, bass.ds(h, 1)].rearrange("a p e n -> p (a e) n"))\
                          .then_inc(S[f"st_in{n % 2}"], 16)

            @block.tensor
            def _(pe):
                pe.wait_ge(S["in_"], ONE + 16)
                with pe.Fori(0, RH) as h:
                    def turn(n):
                        pe.wait_ge(S[f"qkvg{n % 2}"], count(h, 8 * NB, 16 * (n // 2) + 16))
                        pe.wait_ge(S["k_lo"], count(h, NB, n))
                        pe.wait_ge(S["v_lo"], count(h, NB, n))
                        pe.wait_ge(S["gate"], count(h, NB, n))
                        for j in range(2):
                            pe.transpose(kT[:, j * W:(j + 1) * W], cx[:, n % 2, 2 + j, :], ident[:, :])
                        for j in range(4):
                            pe.transpose(vT[:, j * W:(j + 1) * W], cx[:, n % 2, 4 + j, :], ident[:, :])
                        for j in range(4):
                            mm = pe.transpose(gT[:, j * W:(j + 1) * W], cx[:, n % 2, 8 + j, :], ident[:, :])
                        mm.then_inc(S["turned"], 1)

                    def inner(n):
                        pe.wait_ge(S["q_lo"], count(h, NB, n + 1))
                        pe.wait_ge(S["gated"], count(h, NB, max(n - 1, 0)))
                        accumulate(pe, uB[:, 0:W],
                                   [(qkh[:, n % 2, 2 + j, :], qkl[:, n % 2, 2 + j, :], qkh[:, n % 2, j, :], qkl[:, n % 2, j, :])
                                    for j in range(2)])\
                            .then_inc(S["inner"], 1)

                    def output(n):
                        pe.wait_ge(S["inner_lo"], count(h, NB, n + 1))
                        pe.wait_ge(S["v_lo"], count(h, NB, n + 1))
                        pe.wait_ge(S["s_lo"], count(h, NB, n))
                        if n < NB - 1:
                            pe.wait_ge(S["inner_d"], count(h, NB, n + 2))
                        b = n % 2
                        terms = [(ih[:, b, :], il[:, b, :], vh[:, b, :], vl[:, b, :])]
                        if n:
                            terms += [(qkh[:, b, j, :], qkl[:, b, j, :], sh[:, j, :], sl[:, j, :]) for j in range(2)]
                        accumulate(pe, uB[:, :], terms).then_inc(S["out_"], 1)

                    def update(n, j):
                        pe.wait_ge(S["k_lo"], count(h, NB, n + 1))
                        pe.wait_ge(S["state"], count(h, 2 * NB, 2 * n + j))
                        kk = slice(j * W, (j + 1) * W)
                        accumulate(pe, kvB[:, :], [(kdh[:, kk], kdl[:, kk], vh[:, n % 2, :], vl[:, n % 2, :])]).then_inc(S["kv"], 1)

                    def back(n):
                        pe.wait_ge(S["scaled"], count(h, NB, n + 1))
                        pe.wait_ge(S["back_c"], count(h, NB, n))
                        if n == 0:
                            pe.wait_ge(S["x_backc"], ONE + h)
                        for j in range(4):
                            mm = pe.transpose(oT[:, j * W:(j + 1) * W], ga[:, j * W:(j + 1) * W], ident[:, :])
                        mm.then_inc(S["back"], 1)

                    def sample_rows():
                        pe.wait_ge(S["x_in"], ONE + 16 * h + 16)
                        pe.wait_ge(S["x_rows"], ONE + 2 * h)
                        for j in range(4):
                            pe.transpose(sB[0:NS, j * W:(j + 1) * W], xs[:, 4 + j, :], ident[:, :])
                        for j in range(4):
                            mm = pe.transpose(xB[0:NS, j * W:(j + 1) * W], xs[:, 8 + j, :], ident[:, :])
                        mm.then_inc(S["x_turned"], 1)

                    def spread(b):
                        pe.wait_ge(S["x_rows"], ONE + 2 * h + 2)
                        pe.wait_ge(S["outer"], count(h, 2 * NS, 2 * b))
                        pe.matmul(sB[:, :], ident[0:NS, b:b + 1].to_broadcast([NS, P]), xv[:, :], start=True, stop=True).then_inc(S["spread"], 1)

                    def sample_out(b):
                        pe.wait_ge(S["x_mask"], ONE + 2 * h + 2)
                        pe.wait_ge(S["outer"], count(h, 2 * NS, 2 * b + 2))
                        for j in range(2):
                            mm = pe.matmul(xB[0:NS, :], qm[:, j, b, :], s0[:, b % 2, j, :], start=(b == 0 and j == 0),
                                           stop=(b == NS - 1 and j == 1))
                        mm.then_inc(S["x_o"], 1)

                    for n in range(NB + 2):
                        if n < NB:
                            turn(n)
                        if n >= 2:
                            back(n - 2)
                        if n < NB:
                            inner(n)
                        if n == 0:
                            sample_rows()
                        if n < NB:
                            update(n, 0)
                            spread(n)
                            update(n, 1)
                        if 1 <= n <= NB:
                            output(n - 1)
                        if n < NB:
                            sample_out(n)
                    pe.wait_ge(S["x_gated"], ONE + h + 1)
                    pe.wait_ge(S["back_c"], count(h, NB, NB))
                    pe.sem_inc(S["passed"], 1)
                    for j in range(4):
                        mm = pe.transpose(oT[:, j * NS:(j + 1) * NS], xga[:, j * W:(j + 1) * W], ident[0:NS, 0:NS])
                    mm.then_inc(S["x_back"], 1)

            @block.scalar
            def _(act):
                act.wait_ge(S["in_"], ONE + 16)
                with act.Fori(0, RH) as h:
                    act.wait_ge(S["head_in"], ONE + 16 * h + 16)

                    def q_hi(n):
                        act.wait_ge(S[f"qkvg{n % 2}"], count(h, 8 * NB, 16 * (n // 2) + 16))
                        act.wait_ge(S["out_"], count(h, NB, max(n - 1, 0)))
                        act.activation(qkh[:, n % 2, :, :], cx[:, n % 2, 0:4, :], ACT.Copy).then_inc(S["q_hi"], 1)

                    def rows(n):
                        act.wait_ge(S["turned"], count(h, NB, n + 1))
                        act.wait_ge(S["kv"], count(h, 2 * NB, 2 * n))
                        act.wait_ge(S["out_"], count(h, NB, max(n - 1, 0)))
                        act.activation(vh[:, n % 2, :], vT[:, :], ACT.Copy).then_inc(S["v_hi"], 1)
                        act.activation(kdh[:, :], kT[:, 0:RK], ACT.Copy, scale=dec[:, W:W + 1]).then_inc(S["k_hi"], 1)
                        act.wait_ge(S["gated"], count(h, NB, max(n - 1, 0)))
                        act.activation(gt[:, n % 2, :], gT[:, :], ACT.Copy).then_inc(S["gate"], 1)

                    def inner_hi(n):
                        act.wait_ge(S["inner_d"], count(h, NB, n + 1))
                        act.wait_ge(S["out_"], count(h, NB, max(n - 1, 0)))
                        act.activation(ih[:, n % 2, :], inn[:, :], ACT.Copy).then_inc(S["inner_hi"], 1)

                    def root(n):
                        act.wait_ge(S["small"], count(h, 3 * NB, 3 * n + 1))
                        act.activation(st[:, 3:4], st[:, 2:3], ACT.Sqrt).then_inc(S["root"], 1)

                    def scale(n):
                        act.wait_ge(S["gated"], count(h, NB, n + 1))
                        act.wait_ge(S["small"], count(h, 3 * NB, 3 * n + 3))
                        act.activation(ga[:, :], ga[:, :], ACT.Copy, scale=st[:, 5:6]).then_inc(S["scaled"], 1)

                    def back(n):
                        act.wait_ge(S["back"], count(h, NB, n + 1))
                        act.wait_ge(S["o_out"], count(h, 16 * NB, 16 * n))
                        act.activation(ob[:, :, :], oT[:, :].rearrange("p (a n) -> p a n", a=4), ACT.Copy).then_inc(S["back_c"], 1)
                        act.wait_ge(S["back_c"], count(h, NB, n + 1))
                        act.dma_start(A["scr_o"][bass.ds(h * 4, 4)].rearrange("a p n -> p a n")[:, :, n * W:(n + 1) * W],
                                      ob[:, :, :]).then_inc(S["o_out"], 16)

                    def state_hi(n):
                        act.wait_ge(S["state"], count(h, 2 * NB, 2 * n + 2))
                        act.wait_ge(S["out_"], count(h, NB, n + 1))
                        act.activation(sh[:, :, :], state[n % 2], ACT.Copy).then_inc(S["s_hi"], 1)

                    def decay_state(n):
                        act.wait_ge(S[f"st_in{n % 2}"], count(h, 8 * NS, 16 * (n // 2) + 16))
                        act.activation(s0[:, n % 2, :, :], s0[:, n % 2, :, :], ACT.Copy,
                                       scale=dec[:, W + 4:W + 5]).then_inc(S["decay"], 1)

                    q_hi(0)
                    for n in range(NB + 2):
                        if n < NB:
                            rows(n)
                        if n == 0:
                            act.wait_ge(S["x_turned"], ONE + h + 1)
                            act.wait_ge(S["x_gated"], ONE + h)
                            act.activation(xv[:, :], sB[0:NS, :], ACT.Copy).then_inc(S["x_rows"], 1)
                            act.activation(xg[:, :], xB[0:NS, :], ACT.Copy).then_inc(S["x_rows"], 1)
                        if n >= 2:
                            back(n - 2)
                        if n < NB:
                            inner_hi(n)
                        if n == 0:
                            decay_state(0)
                        if n < NB - 1:
                            decay_state(n + 1)
                        if 1 <= n <= NB:
                            state_hi(n - 1)
                        if n < NB - 1:
                            q_hi(n + 1)
                        if n < NB:
                            act.wait_ge(S["outer"], count(h, 2 * NS, 2 * n + 2))
                            act.dma_start(A["state_s"][n, bass.ds(h, 1)].rearrange("a p e n -> p (a e) n"),
                                          s0[:, n % 2, :, :]).then_inc(S[f"st_out{n % 2}"], 16)
                        if 1 <= n <= NB:
                            root(n - 1)
                            scale(n - 1)
                    act.dma_start(A["state_p"][bass.ds(h, 1)].rearrange("a p e n -> p (a e) n"),
                                  state[(NB - 1) % 2]).then_inc(S["s_out"], 16)
                    act.wait_ge(S["x_small"], ONE + 4 * h + 2)
                    act.activation(xst[:, 3:4], xst[:, 2:3], ACT.Sqrt).then_inc(S["x_root"], 1)
                    act.wait_ge(S["x_back"], ONE + h + 1)
                    act.wait_ge(S["x_out"], ONE + 16 * h)
                    act.activation(xo[:, :, :], oT[:, 0:4 * NS].rearrange("p (a n) -> p a n", a=4), ACT.Copy).then_inc(S["x_backc"], 1)
                    act.wait_ge(S["x_backc"], ONE + h + 1)
                    act.dma_start(A["scr_o"][bass.ds(h * 4, 4)].rearrange("a p n -> p a n")[:, :, SEQ:TOK],
                                  xo[:, :, :]).then_inc(S["x_out"], 16)
                act.wait_ge(S["o_out"], ONE + 16 * NB * RH)
                act.wait_ge(S["x_out"], ONE + 16 * RH)
                act.wait_ge(S["s_out"], ONE + 16 * RH)
                act.wait_ge(S["st_out0"], ONE + 8 * NS * RH)
                act.wait_ge(S["st_out1"], ONE + 8 * NS * RH)

            @block.vector
            def _(dve):
                dve.wait_ge(S["in_"], ONE + 16)
                with dve.Fori(0, RH) as h:
                    dve.wait_ge(S["head_in"], ONE + 16 * h + 16)

                    def rows(n):
                        dve.wait_ge(S["v_hi"], count(h, NB, n + 1))
                        dve.tensor_tensor(vl[:, n % 2, :], vT[:, :], vh[:, n % 2, :].bitcast(F32), ALU.subtract).then_inc(S["v_lo"], 1)
                        dve.wait_ge(S["k_hi"], count(h, NB, n + 1))
                        dve.scalar_tensor_tensor(kdl[:, :], kT[:, 0:RK], dec[:, W:W + 1], kdh[:, :].bitcast(F32),
                                                 ALU.mult, ALU.subtract).then_inc(S["k_lo"], 1)

                    def decay(n):
                        dve.wait_ge(S["inner"], count(h, NB, n + 1))
                        dve.wait_ge(S["inner_lo"], count(h, NB, n))
                        dve.tensor_tensor(inn[:, :], uB[:, 0:W], dec[:, 0:W], ALU.mult).then_inc(S["inner_d"], 1)
                        dve.wait_ge(S["inner_hi"], count(h, NB, n + 1))
                        dve.tensor_tensor(il[:, n % 2, :], inn[:, :], ih[:, n % 2, :].bitcast(F32), ALU.subtract).then_inc(S["inner_lo"], 1)

                    def norm(n):
                        dve.wait_ge(S["out_"], count(h, NB, n + 1))
                        dve.bn_stats(st6[:, :], uB[:, :]).then_inc(S["stats"], 1)
                        dve.wait_ge(S["stats"], count(h, 2 * NB, 2 * n + 1))
                        dve.wait_ge(S["scaled"], count(h, NB, n))
                        dve.sem_inc(S["passed"], 1)
                        dve.bn_aggr(st[:, 0:2], st6[:, :]).then_inc(S["stats"], 1)
                        dve.wait_ge(S["stats"], count(h, 2 * NB, 2 * n + 2))
                        dve.tensor_scalar(st[:, 2:3], st[:, 1:2], dec[:, W + 1:W + 2], EPS, ALU.mult, ALU.add).then_inc(S["small"], 1)
                        dve.wait_ge(S["gate"], count(h, NB, n + 1))
                        dve.wait_ge(S["back"], count(h, NB, n))
                        dve.scalar_tensor_tensor(ga[:, :], uB[:, :], st[:, 0:1], gt[:, n % 2, :], ALU.subtract, ALU.mult)\
                           .then_inc(S["gated"], 1)

                    def norm_rest(n):
                        dve.wait_ge(S["root"], count(h, NB, n + 1))
                        dve.reciprocal(st[:, 4:5], st[:, 3:4]).then_inc(S["small"], 1)
                        dve.wait_ge(S["small"], count(h, 3 * NB, 3 * n + 2))
                        dve.tensor_scalar(st[:, 5:6], st[:, 4:5], dec[:, W + 2:W + 3], None, ALU.mult).then_inc(S["small"], 1)

                    def update(n, j):
                        dve.wait_ge(S["kv"], count(h, 2 * NB, 2 * n + j + 1))
                        if j == 0:
                            dve.wait_ge(S["s_lo"], count(h, NB, max(n - 1, 0)))
                        if n == 1 and j == 0:
                            dve.wait_ge(S["s_out"], ONE + 16 * h)
                        if n:
                            dve.scalar_tensor_tensor(state[n % 2][:, j, :], state[(n - 1) % 2][:, j, :], dec[:, W + 3:W + 4],
                                                     kvB[:, :], ALU.mult, ALU.add).then_inc(S["state"], 1)
                        else:
                            dve.tensor_copy(state[0][:, j, :], kvB[:, :]).then_inc(S["state"], 1)

                    def outer(b):
                        dve.wait_ge(S["spread"], count(h, NS, b + 1))
                        dve.wait_ge(S["decay"], count(h, NS, b + 1))
                        for j in range(2):
                            dve.scalar_tensor_tensor(s0[:, b % 2, j, :], sB[:, :], k16[:, j, b:b + 1], s0[:, b % 2, j, :],
                                                     ALU.mult, ALU.add).then_inc(S["outer"], 1)

                    def masks():
                        dve.wait_ge(S["x_in"], ONE + 16 * h + 16)
                        dve.wait_ge(S["x_o"], count(h, NS, 0))
                        for j in range(2):
                            a = dve.tensor_tensor(qm[:, j, :, :], m8[:, :, :], xs[:, j:j + 1, :].to_broadcast([P, NS, NS]), ALU.mult)
                        a.then_inc(S["x_mask"], 1)
                        dve.tensor_scalar(k16[:, :, :], xs[:, 2:4, :], RK ** -0.5, None, ALU.mult).then_inc(S["x_mask"], 1)
                        dve.wait_ge(S["x_mask"], ONE + 2 * h + 2)

                    for n in range(NB + 1):
                        if n < NB:
                            rows(n)
                            decay(n)
                        if n == 0:
                            masks()
                        if n < NB:
                            update(n, 0)
                            update(n, 1)
                            outer(n)
                        if n:
                            norm(n - 1)
                            norm_rest(n - 1)
                    dve.wait_ge(S["x_o"], count(h, NS, NS))
                    dve.bn_stats(xst6[:, :], xB[0:NS, :]).then_inc(S["x_stats"], 1)
                    dve.wait_ge(S["x_stats"], ONE + 2 * h + 1)
                    dve.sem_inc(S["passed"], 1)
                    dve.bn_aggr(xst[:, 0:2], xst6[:, :]).then_inc(S["x_stats"], 1)
                    dve.wait_ge(S["x_stats"], ONE + 2 * h + 2)
                    dve.tensor_scalar(xst[:, 6:7], xst[:, 0:1], -1.0, None, ALU.mult).then_inc(S["x_small"], 1)
                    dve.tensor_scalar(xst[:, 2:3], xst[:, 1:2], EPS, None, ALU.add).then_inc(S["x_small"], 1)
                    dve.wait_ge(S["x_root"], ONE + h + 1)
                    dve.reciprocal(xst[:, 4:5], xst[:, 3:4]).then_inc(S["x_small"], 1)
                    dve.wait_ge(S["x_back"], ONE + h)
                    dve.wait_ge(S["x_small"], ONE + 4 * h + 3)
                    dve.tensor_scalar(xga[:, :], xB[0:NS, :], xst[:, 0:1], xst[:, 4:5], ALU.subtract, ALU.mult).then_inc(S["x_small"], 1)
                    dve.wait_ge(S["x_small"], ONE + 4 * h + 4)
                    dve.tensor_tensor(xga[:, :], xga[:, :], xg[:, :], ALU.mult).then_inc(S["x_gated"], 1)

            @block.gpsimd
            def _(pool):
                pool.wait_ge(S["in_"], ONE + 16)
                with pool.Fori(0, RH) as h:
                    pool.wait_ge(S["head_in"], ONE + 16 * h + 16)
                    def q_lo(n):
                        pool.wait_ge(S["q_hi"], count(h, NB, n + 1))
                        pool.tensor_tensor(qkl[:, n % 2, :, :], cx[:, n % 2, 0:4, :], qkh[:, n % 2, :, :].bitcast(F32),
                                           ALU.subtract).then_inc(S["q_lo"], 1)

                    q_lo(0)
                    q_lo(1)
                    for n in range(NB):
                        pool.wait_ge(S["s_hi"], count(h, NB, n + 1))
                        pool.tensor_tensor(sl[:, :, :], state[n % 2], sh[:, :, :].bitcast(F32), ALU.subtract).then_inc(S["s_lo"], 1)
                        if n < NB - 2:
                            q_lo(n + 2)


def retention_out(nc, A, env):
    ctx, sem, bank = env["ctx"], env["sem"], env["bank"]
    y, jobs, lo_done = env["y"], env["jobs"], env["lo_done"]
    load_slab, split_hi, split_lo = env["load_slab"], env["split_hi"], env["split_lo"]
    columns, down_job = env["columns"], env["down_job"]
    S = {n: sem("o_" + n) for n in SEMS["o_"]}
    NO = 8
    with ExitStack() as c:
        def sb(name, shape, dt=F32):
            return c.enter_context(nc.sbuf_tensor("o_" + name, shape, dt))
        of = sb("of", [P, 2, 2, TOK])
        oh = sb("oh", [P, 2, 2, TOK], F32R)
        ol = sb("ol", [P, 2, 2, TOK], F32R)
        with nc.Block() as block:
            @block.sync
            def _(sp):
                for n in range(NO + 1):
                    if n < NO:
                        if n >= 2:
                            sp.wait_ge(S["lo"], ONE + n - 1)
                        sp.dma_start(of[:, n % 2, :, :], A["scr_o"][2 * n:2 * n + 2].rearrange("a p n -> p a n")).then_inc(S[f"in{n % 2}"], 16)
                    if n:
                        for j in range(2):
                            load_slab(sp, S_RO + AHEAD + 2 * (n - 1) + j)

            @block.tensor
            def _(pe):
                for n in range(NO):
                    pe.wait_ge(lo_done, ONE + S_RO + 2 * n + 2)
                    pe.wait_ge(S["lo"], ONE + n + 1)
                    for q in range(DOWN_J):
                        ft, ch = divmod(q, NCH)
                        if n * DOWN_J + q >= 8:
                            pe.wait_ge(S["yadd"], ONE + n * DOWN_J + q - 7)
                        down_job(pe, bank[q % 8][:, 0:CH], S_RO + 2 * n, ft, ch, oh[:, n % 2, :, :], ol[:, n % 2, :, :])\
                            .then_inc(jobs, 1)

            @block.scalar
            def _(act):
                for n in range(NO + 1):
                    if n < NO:
                        act.wait_ge(S[f"in{n % 2}"], ONE + 16 * (n // 2) + 16)
                        if n >= 2:
                            act.wait_ge(jobs, ONE + J_RO + DOWN_J * (n - 1))
                        act.activation(oh[:, n % 2, :, :], of[:, n % 2, :, :], ACT.Copy).then_inc(S["hi"], 1)
                    if n:
                        for j in range(2):
                            split_hi(act, S_RO + AHEAD + 2 * (n - 1) + j)

            @block.vector
            def _(dve):
                for n in range(NO):
                    for q in range(DOWN_J):
                        ft, ch = divmod(q, NCH)
                        dve.wait_ge(jobs, ONE + J_RO + DOWN_J * n + q + 1)
                        dve.tensor_tensor(y[:, ft, columns(ch)], bank[q % 8][:, 0:CH], y[:, ft, columns(ch)],
                                          ALU.add).then_inc(S["yadd"], 1)
                    for j in range(2):
                        split_lo(dve, S_RO + AHEAD + 2 * n + j)

            @block.gpsimd
            def _(pool):
                for n in range(NO):
                    pool.wait_ge(S["hi"], ONE + n + 1)
                    if n >= 2:
                        pool.wait_ge(jobs, ONE + J_RO + DOWN_J * (n - 1))
                    pool.tensor_tensor(ol[:, n % 2, :, :], of[:, n % 2, :, :], oh[:, n % 2, :, :].bitcast(F32),
                                       ALU.subtract).then_inc(S["lo"], 1)


def tables():
    f = np.float32
    pos = np.concatenate([np.arange(SEQ), np.full(NS, SEQ)]).astype(f)
    half = HD // 2
    inv = (f(10000.0) ** (-np.arange(half, dtype=f) / f(half))).astype(f)
    ang = (np.concatenate([np.arange(SEQ), np.full(P, SEQ)]).astype(f)[:, None] * inv[None, :]).astype(f)

    def by_block(t):
        return np.ascontiguousarray(t.astype(f).reshape(NB + 1, P, half).transpose(1, 0, 2))
    ca = np.cos(ang.astype(np.float64))
    sa = np.sin(ang.astype(np.float64))
    angle = (f(1.0) / (f(10000.0) ** np.linspace(0.0, 1.0, RK // 2, dtype=f))).astype(f)
    angr = (angle[:, None] * pos[None, :]).astype(f).astype(np.float64)
    i = np.arange(W)
    mask = np.zeros((P, 2 * W), f)
    mask[:, :W][i[None, :] < i[:, None]] = NEG
    mask[:, W:][i[None, :] > i[:, None]] = NEG
    dec = np.zeros((RH, P, W + 5), f)
    for h in range(RH):
        lg = np.log1p(-(2.0 ** (-5.0 - h)))
        inner = np.exp(-lg * (i + 1.0))[:, None] * (i[:, None] <= i[None, :]) * RK ** -0.5
        dec[h, :, 0:W] = inner
        dec[h, :, W] = np.exp(lg * (W - 1.0 - i)) * RK ** -0.5
        dec[h, :, W + 1] = np.exp(2 * lg * (i + 1.0))
        dec[h, :, W + 2] = np.exp(lg * (i + 1.0))
        dec[h, :, W + 3] = np.exp(lg * W)
        dec[h, :, W + 4] = np.exp(lg)
    eye = np.eye(NS, dtype=f)
    return {
        "ident": np.eye(P, dtype=f), "ones": np.full((P, P), 1.0 / D, f),
        "cosT": by_block(ca), "sinT": by_block(sa), "mask": mask,
        "cosR": np.cos(angr).astype(f), "sinR": np.sin(angr).astype(f), "dec": dec,
        "same": np.repeat(eye, GH, axis=0),
        "m8": np.repeat(eye[None], P, axis=0),
    }


def kernel(**inputs):
    import concourse.bacc as bacc
    from concourse.bass_utils import run_bass_kernel_spmd

    a = {n: np.asarray(v) for n, v in inputs.items()}

    def up_slabs(w, starts):
        return [w[:, s:s + P].reshape(KT, P, P).transpose(1, 0, 2).reshape(P, SLAB) for s in starts]

    qkv, wo = a["attn_w_qkv"][0], a["attn_w_o"][0]
    rin, ro = a["ret_w_in"][0], a["ret_w_o"][0]
    slabs = []
    for g in range(NG):
        cols = np.concatenate([qkv[:, g * 256:(g + 1) * 256], qkv[:, D + g * HD:D + (g + 1) * HD],
                               qkv[:, D + 256 + g * HD:D + 256 + (g + 1) * HD]], axis=1)
        slabs += up_slabs(cols, (0, P, 2 * P))
        slabs += [wo[g * 256:g * 256 + P], wo[g * 256 + P:(g + 1) * 256]]

    def ffn(layer):
        wi, wo_ = a["ffn_w_in"][layer], a["ffn_w_out"][layer]
        out = []
        for n in range(NBLK + 1):
            if n < NBLK:
                out += up_slabs(wi, (2 * n * P, FF + 2 * n * P, (2 * n + 1) * P, FF + (2 * n + 1) * P))
            if n:
                out += [wo_[(2 * n - 2 + j) * P:(2 * n - 1 + j) * P] for j in range(2)]
        return out
    slabs += ffn(0)
    for h in range(RH):
        for part in range(2):
            w = rin[:, part * D + h * RK:part * D + (h + 1) * RK]
            slabs += up_slabs(w[:, 0::2], (0,)) + up_slabs(w[:, 1::2], (0,))
        for part in range(2):
            s = 2 * D + part * RH * RV + h * RV
            slabs += up_slabs(rin, range(s, s + RV, P))
    slabs += [ro[n * P:(n + 1) * P] for n in range(16)]
    slabs += ffn(1)

    def tiles(v, n):
        return np.moveaxis(v.reshape(v.shape[:-1] + (n, P)), -1, 0)

    x = np.concatenate([a["x_prompt"][0], a["x_sample"][:, 0]], axis=0)
    taps = np.concatenate([a["ffn_conv_w"], a["ffn_conv_b"][:, None]], axis=1)
    ins = {
        "w": np.stack(slabs),
        "x": x.T.reshape(KT, P, TOK).transpose(1, 0, 2),
        "kcache": a["cache_k_win"][0].transpose(2, 3, 0, 1),
        "vcache": a["cache_v_win"][0].transpose(2, 1, 0, 3),
        "kcache_rows": a["cache_k_win"][0],
        "vcache_rows": a["cache_v_win"][0],
        "sinkb": np.repeat(a["attn_sinks"], P, axis=0),
        "sinkc": np.tile(a["attn_sinks"][0].reshape(NG, GH).T, (NS, 1)),
        "state_in": a["state_ret"][0].reshape(NS, RH, P, 2, RV),
        "past": np.stack([a["state_conv"][n].transpose(2, 1, 0).reshape(FT, P, 2, NS).transpose(1, 0, 2, 3) for n in range(2)]),
        "taps": np.stack([tiles(taps[n], FT).transpose(0, 2, 1).reshape(P, FT * 4) for n in range(2)]),
        "ln_mix": np.stack([tiles(np.stack([a["ln_mix_g"][n], a["ln_mix_b"][n]]), KT) for n in range(2)]),
        "ln_ffn": np.stack([tiles(np.stack([a["ln_ffn_g"][n], a["ln_ffn_b"][n]]), KT) for n in range(2)]),
        **tables(),
    }
    ins = {n: np.ascontiguousarray(v) for n, v in ins.items()}
    outs = {
        "y": (P, KT, TOK), "kwin_p": (W, NG, HD), "vwin_p": (W, NG, HD), "kwin_s": (NS, W, NG, HD),
        "vwin_s": (NS, W, NG, HD), "state_p": (RH, P, 2, RV), "state_s": (NS, RH, P, 2, RV),
        "conv_rows": (2, P, FT * 10), "conv_past": (2, P, FT, NS),
    }
    nc = bacc.Bacc("TRN2", target_bir_lowering=False, num_devices=1, dynamic_dma_scratch_size=512)
    A = {n: nc.dram_tensor("in_" + n, v.shape, F32, kind="ExternalInput").ap() for n, v in ins.items()}
    A |= {n: nc.dram_tensor("out_" + n, s, F32, kind="ExternalOutput").ap() for n, s in outs.items()}
    A["scr"] = nc.dram_tensor("scratch_qkvg", (12 * RH, P, TOK), F32, kind="Internal").ap()
    A["scr_o"] = nc.dram_tensor("scratch_heads", (16, P, TOK), F32, kind="Internal").ap()
    build(nc, A)
    r = run_bass_kernel_spmd(nc, [{"in_" + n: v for n, v in ins.items()}], core_ids=[0]).results[0]
    r = {n: np.asarray(r["out_" + n]) for n in outs}

    yt = r["y"].transpose(1, 0, 2).reshape(D, TOK).T
    rows = r["conv_rows"].reshape(2, P, FT, 10).transpose(0, 3, 2, 1).reshape(2, 10, FF)
    past = r["conv_past"].transpose(0, 3, 2, 1).reshape(2, NS, FF)
    return (np.ascontiguousarray(yt[:SEQ])[None], np.ascontiguousarray(yt[SEQ:])[:, None],
            r["kwin_p"][None, None], r["vwin_p"][None, None],
            r["state_p"].reshape(1, 1, RH, RK, RV),
            np.ascontiguousarray(rows[:, None, 0:2]),
            r["kwin_s"][None], r["vwin_s"][None],
            r["state_s"].reshape(1, NS, RH, RK, RV),
            np.stack([past, rows[:, 2:]], axis=2))
```
